# Optimizing a Trainium2 kernel written in Bass

```python
import math
import jax, jax.numpy as jnp
from jax import lax
import numpy as np

D_MODEL = 2048
BATCH = 1
SEQ = 512
DEPTH = 1

S5_WIDTH = D_MODEL // 4
S5_GROUP = 16
S5_GROUPS = S5_WIDTH // S5_GROUP
S5_STATE = 64
S5_DT_MIN = 1e-3
S5_DT_MAX = 1e-1
POOL_WIDTH = D_MODEL // 4
POOL_WINDOWS = (2, 4, 8, 16)
POOL_NGROUPS = len(POOL_WINDOWS)
POOL_GROUP = POOL_WIDTH // POOL_NGROUPS
GLA_HEADS = 4
GLA_V_WIDTH = D_MODEL // 2
GLA_K_WIDTH = GLA_V_WIDTH // 2
GLA_DK = GLA_K_WIDTH // GLA_HEADS
GLA_DV = GLA_V_WIDTH // GLA_HEADS
GLA_GATE_RANK = 16
GLA_TAU = 16.0
GLA_CHUNK = 64
MIX_WIDTH = S5_WIDTH + POOL_WIDTH + GLA_V_WIDTH
IN_SPLITS = (S5_WIDTH, POOL_WIDTH, GLA_K_WIDTH, GLA_K_WIDTH, GLA_V_WIDTH, GLA_GATE_RANK, GLA_V_WIDTH)
IN_WIDTH = sum(IN_SPLITS)
D_FF = 5632
CONV_WIDTH = 3
PLE_DIM = 256
EPS = 1e-6

kernel_name = "hymba_s5_pool_gla_hybrid"

def rmsnorm(x, w):
    xf = x.astype(jnp.float32)
    y = xf * lax.rsqrt(jnp.mean(xf * xf, axis=-1, keepdims=True) + EPS) * w.astype(jnp.float32)
    return y.astype(x.dtype)

def _linear_recurrence_op(e1, e2):
    a1, b1 = e1
    a2, b2 = e2
    return a1 * a2, a2 * b1 + b2

def s5_mixer(u, a_re, a_im, log_dt, b_re, b_im, c_re, c_im, d_skip, w_glu, b_glu):
    bsz, L, _ = u.shape
    uf = u.astype(jnp.float32).reshape(bsz, L, S5_GROUPS, S5_GROUP)
    A = lax.complex(a_re.astype(jnp.float32), a_im.astype(jnp.float32))
    dt = jnp.exp(log_dt.astype(jnp.float32))[:, None]
    A_bar = jnp.exp(A * dt)
    Bm = lax.complex(b_re.astype(jnp.float32), b_im.astype(jnp.float32))
    B_bar = ((A_bar - 1.0) / A)[..., None] * Bm
    Bu = jnp.einsum('blgc,gnc->blgn', uf.astype(jnp.complex64), B_bar)
    a = jnp.broadcast_to(A_bar, Bu.shape)
    _, states = lax.associative_scan(_linear_recurrence_op, (a, Bu), axis=1)
    Cm = lax.complex(c_re.astype(jnp.float32), c_im.astype(jnp.float32))
    y = jnp.einsum('blgn,gcn->blgc', states, Cm).real
    y = y + d_skip.astype(jnp.float32).reshape(S5_GROUPS, S5_GROUP) * uf
    y = jax.nn.gelu(y.reshape(bsz, L, S5_WIDTH))
    glu = jax.nn.sigmoid(y @ w_glu.astype(jnp.float32) + b_glu.astype(jnp.float32))
    return (y * glu).astype(u.dtype)

def pool_mixer(z, w_pool, pool_scale):
    bsz, L, _ = z.shape
    zf = z.astype(jnp.float32).reshape(bsz, L, POOL_NGROUPS, POOL_GROUP)
    csum = lax.cumsum(zf, axis=1)
    cpad = jnp.pad(csum, ((0, 0), (1, 0), (0, 0), (0, 0)))
    pos = jnp.arange(1, L + 1, dtype=jnp.float32)[None, :, None]
    outs = []
    for gi, w in enumerate(POOL_WINDOWS):
        hi = cpad[:, 1:, gi]
        lo = jnp.pad(cpad[:, :L + 1 - w, gi], ((0, 0), (w - 1, 0), (0, 0)))
        count = jnp.minimum(pos, float(w))
        outs.append((hi - lo) / count)
    pooled = jnp.stack(outs, axis=2) - zf
    mixed = jnp.einsum('blgc,gcd->blgd', pooled, w_pool.astype(jnp.float32))
    mixed = mixed.reshape(bsz, L, POOL_WIDTH) * pool_scale.astype(jnp.float32)
    return mixed.astype(z.dtype)

def gla_chunked(q, k, v, g):
    bsz, L, H, dk = q.shape
    dv = v.shape[-1]
    n = L // GLA_CHUNK

    def to_chunks(t):
        return t.reshape(bsz, n, GLA_CHUNK, H, t.shape[-1]).transpose(0, 3, 1, 2, 4)

    q, k, v, g = to_chunks(q) * (dk ** -0.5), to_chunks(k), to_chunks(v), to_chunks(g)
    b = jnp.cumsum(g, axis=3)
    b_last = b[:, :, :, -1:, :]
    q_dec = q * jnp.exp(b)
    k_dec = k * jnp.exp(-b)
    scores = jnp.einsum('bhntd,bhnsd->bhnts', q_dec, k_dec)
    causal = jnp.tril(jnp.ones((GLA_CHUNK, GLA_CHUNK), dtype=bool))
    scores = jnp.where(causal, scores, 0.0)
    o_intra = jnp.einsum('bhnts,bhnsv->bhntv', scores, v)
    kv_chunk = jnp.einsum('bhnsd,bhnsv->bhndv', k * jnp.exp(b_last - b), v)
    chunk_decay = jnp.exp(b_last[:, :, :, 0, :])

    def step(S, inp):
        dec, kv_n = inp
        return dec[..., None] * S + kv_n, S

    S0 = jnp.zeros((bsz, H, dk, dv), dtype=jnp.float32)
    _, S_prev = lax.scan(step, S0, (chunk_decay.transpose(2, 0, 1, 3), kv_chunk.transpose(2, 0, 1, 3, 4)))
    S_prev = S_prev.transpose(1, 2, 0, 3, 4)
    o_inter = jnp.einsum('bhntd,bhndv->bhntv', q_dec, S_prev)
    o = o_intra + o_inter
    return o.transpose(0, 2, 3, 1, 4).reshape(bsz, L, H, dv)

def gla_mixer(q, k, v, g_lr, r, w_a2, b_a, norm_w):
    bsz, L, _ = q.shape
    f32 = jnp.float32
    qh = q.astype(f32).reshape(bsz, L, GLA_HEADS, GLA_DK)
    kh = k.astype(f32).reshape(bsz, L, GLA_HEADS, GLA_DK)
    vh = v.astype(f32).reshape(bsz, L, GLA_HEADS, GLA_DV)
    logit = g_lr.astype(f32) @ w_a2.astype(f32) + b_a.astype(f32)
    log_alpha = (jax.nn.log_sigmoid(logit) / GLA_TAU).reshape(bsz, L, GLA_HEADS, GLA_DK)
    o = gla_chunked(qh, kh, vh, log_alpha)
    o = rmsnorm(o, norm_w).reshape(bsz, L, GLA_V_WIDTH)
    return (o * jax.nn.silu(r.astype(f32))).astype(q.dtype)

def conv_glu_ffn(a, w_up, conv_w, conv_b, w_down):
    L = a.shape[1]
    up = a @ w_up
    gate, val = up[..., :D_FF], up[..., D_FF:]
    gp = jnp.pad(gate, ((0, 0), (CONV_WIDTH - 1, 0), (0, 0)))
    gc = conv_b
    for j in range(CONV_WIDTH):
        gc = gc + gp[:, j:j + L] * conv_w[j]
    return (jax.nn.silu(gc) * val) @ w_down

def setup_inputs(seed: int = 0) -> dict:
    key = jax.random.key(seed)
    ks = jax.random.split(key, 32)
    f32 = jnp.float32

    def nrm(k, shape, scale):
        return jax.random.normal(k, shape, f32) * scale

    def gain(k, shape):
        return 1.0 + 0.02 * jax.random.normal(k, shape, f32)

    n_idx = jnp.arange(S5_STATE, dtype=f32)
    a_re = -0.5 + 0.01 * jax.random.normal(ks[4], (DEPTH, S5_GROUPS, S5_STATE), f32)
    a_im = math.pi * n_idx + 0.01 * jax.random.normal(ks[5], (DEPTH, S5_GROUPS, S5_STATE), f32)
    log_dt = jax.random.uniform(ks[6], (DEPTH, S5_GROUPS), f32, math.log(S5_DT_MIN), math.log(S5_DT_MAX))
    return {
        "x": nrm(ks[0], (BATCH, SEQ, D_MODEL), 1.0),
        "p": nrm(ks[1], (DEPTH, BATCH, SEQ, PLE_DIM), 1.0),
        "norm_mix_w": gain(ks[2], (DEPTH, D_MODEL)),
        "w_in": nrm(ks[3], (DEPTH, D_MODEL, IN_WIDTH), D_MODEL ** -0.5),
        "s5_a_re": a_re,
        "s5_a_im": a_im,
        "s5_log_dt": log_dt,
        "s5_b_re": nrm(ks[7], (DEPTH, S5_GROUPS, S5_STATE, S5_GROUP), (2 * S5_GROUP) ** -0.5),
        "s5_b_im": nrm(ks[8], (DEPTH, S5_GROUPS, S5_STATE, S5_GROUP), (2 * S5_GROUP) ** -0.5),
        "s5_c_re": nrm(ks[9], (DEPTH, S5_GROUPS, S5_GROUP, S5_STATE), S5_STATE ** -0.5),
        "s5_c_im": nrm(ks[10], (DEPTH, S5_GROUPS, S5_GROUP, S5_STATE), S5_STATE ** -0.5),
        "s5_d": nrm(ks[11], (DEPTH, S5_WIDTH), 1.0),
        "s5_w_glu": nrm(ks[12], (DEPTH, S5_WIDTH, S5_WIDTH), S5_WIDTH ** -0.5),
        "s5_b_glu": nrm(ks[13], (DEPTH, S5_WIDTH), 0.02),
        "pool_w": nrm(ks[14], (DEPTH, POOL_NGROUPS, POOL_GROUP, POOL_GROUP), POOL_GROUP ** -0.5),
        "pool_scale": gain(ks[15], (DEPTH, POOL_WIDTH)),
        "gla_w_a2": nrm(ks[16], (DEPTH, GLA_GATE_RANK, GLA_K_WIDTH), GLA_GATE_RANK ** -0.5),
        "gla_b_a": nrm(ks[17], (DEPTH, GLA_K_WIDTH), 0.1),
        "gla_norm_w": gain(ks[18], (DEPTH, GLA_DV)),
        "w_out": nrm(ks[19], (DEPTH, MIX_WIDTH, D_MODEL), MIX_WIDTH ** -0.5),
        "norm_ffn_w": gain(ks[20], (DEPTH, D_MODEL)),
        "w_up": nrm(ks[21], (DEPTH, D_MODEL, 2 * D_FF), D_MODEL ** -0.5),
        "conv_w": nrm(ks[22], (DEPTH, CONV_WIDTH, D_FF), CONV_WIDTH ** -0.5),
        "conv_b": nrm(ks[23], (DEPTH, D_FF), 0.02),
        "w_down": nrm(ks[24], (DEPTH, D_FF, D_MODEL), D_FF ** -0.5),
        "norm_ple_w": gain(ks[25], (DEPTH, D_MODEL)),
        "w_ple": nrm(ks[26], (DEPTH, PLE_DIM, D_MODEL), PLE_DIM ** -0.5),
        "w_pg": nrm(ks[27], (DEPTH, D_MODEL, D_MODEL), D_MODEL ** -0.5),
        "final_norm_w": gain(ks[28], (D_MODEL,)),
    }

def reference(x, p, norm_mix_w, w_in, s5_a_re, s5_a_im, s5_log_dt, s5_b_re, s5_b_im, s5_c_re, s5_c_im,
              s5_d, s5_w_glu, s5_b_glu, pool_w, pool_scale, gla_w_a2, gla_b_a, gla_norm_w, w_out,
              norm_ffn_w, w_up, conv_w, conv_b, w_down, norm_ple_w, w_ple, w_pg, final_norm_w):
    h = x
    split_at = list(np.cumsum(IN_SPLITS)[:-1])
    for i in range(DEPTH):
        a = rmsnorm(h, norm_mix_w[i])
        z = a @ w_in[i]
        u_s5, z_pool, q, k, v, g_lr, r = jnp.split(z, split_at, axis=-1)
        y_s5 = s5_mixer(u_s5, s5_a_re[i], s5_a_im[i], s5_log_dt[i], s5_b_re[i], s5_b_im[i],
                        s5_c_re[i], s5_c_im[i], s5_d[i], s5_w_glu[i], s5_b_glu[i])
        y_pool = pool_mixer(z_pool, pool_w[i], pool_scale[i])
        y_gla = gla_mixer(q, k, v, g_lr, r, gla_w_a2[i], gla_b_a[i], gla_norm_w[i])
        mixed = jnp.concatenate([y_s5, y_pool, y_gla], axis=-1)
        h = h + (mixed @ w_out[i]).astype(h.dtype)
        f = conv_glu_ffn(rmsnorm(h, norm_ffn_w[i]), w_up[i], conv_w[i], conv_b[i], w_down[i])
        h = h + f.astype(h.dtype)
        gate = jax.nn.sigmoid(rmsnorm(h, norm_ple_w[i]) @ w_pg[i])
        h = h + ((p[i] @ w_ple[i]) * gate).astype(h.dtype)
    return rmsnorm(h, final_norm_w)


_drawn_inputs = setup_inputs


def setup_inputs(seed=0):
    import zlib

    import numpy as np

    out = dict(_drawn_inputs(seed))
    spreads = {}
    factors = {'norm_mix_w': 3.201,
     's5_a_re': 64.0,
     's5_a_im': 32.92,
     's5_log_dt': 33.576,
     's5_b_re': 46.44,
     's5_b_im': 45.712,
     's5_c_re': 46.304,
     's5_c_im': 46.232,
     's5_b_glu': 200.0,
     'pool_scale': 80.459,
     'gla_b_a': 3.683,
     'gla_norm_w': 72.27,
     'norm_ffn_w': 13.673,
     'conv_b': 19.309,
     'norm_ple_w': 200.0,
     'final_norm_w': 20.312,
     'w_pg': 22.2,
     'p': 8.0,
     's5_d': 3.597,
     's5_w_glu': 6.246,
     'w_ple': 8.0}
    for name, (base, spread) in spreads.items():
        noise = np.random.default_rng([zlib.crc32(name.encode()), seed]).standard_normal(out[name].shape)
        drawn = base * np.exp(spread * noise) if base else spread * noise
        out[name] = __import__('jax').numpy.asarray(drawn.astype(out[name].dtype))
    for name, factor in factors.items():
        out[name] = (out[name] * factor).astype(out[name].dtype)
    return out
```

```python
from contextlib import ExitStack, contextmanager
import math

import concourse.bass as bass
from concourse import mybir

P = 128
SEQ = 512
D = 2048
KT = D // P
D_FF = 5632
FT = D_FF // P
QUARTERS = 4
QT = FT // QUARTERS
PLE_KT = 2
EPS = 1e-6

S5_TILES = 4
PAIRS = 16
STATES = 64
POOL_TILES = 4
HEADS = 4
CHUNK = 64
CHUNKS = SEQ // CHUNK
DV = 256
RANK = 16

N_U, N_Q, N_K, N_G, N_V, N_POOL, N_R = 0, 4, 8, 12, 13, 21, 25
IN_TILES = 33
OUT0 = IN_TILES
FFN0 = OUT0 + KT
UP = 2 * QT
PER_QUARTER = UP + KT
PLE0 = FFN0 + QUARTERS * PER_QUARTER
PG0 = PLE0 + 2
PLE_PER = KT // 2

BU_SLOT = 5
READ_SLOT = 7
HEAD_SLOT = 23

PC = {}
_at = 0
for _name, _n in (("mix", KT), ("ffn", KT), ("ple", KT), ("final", KT), ("d", 4), ("b_glu", 4), ("pscale", 4),
                  ("b_a", 4), ("gla_w", 2), ("conv_b", FT), ("conv_w", 3 * FT), ("a_re", PAIRS),
                  ("a_im", PAIRS), ("log_dt", PAIRS)):
    PC[_name] = _at
    _at += _n
N_PARAMS = _at
CC = {}
_at = 0
for _name, _n in (("ident", P), ("corr", POOL_TILES * 16)):
    CC[_name] = _at
    _at += _n
N_CONSTS = _at

TWO_PI = 2.0 * math.pi
INV_2PI = 1.0 / TWO_PI
PI2_A = 6.28125
PI2_B = round((TWO_PI - PI2_A) * 2 ** 20) / 2 ** 20
PI2_C = TWO_PI - PI2_A - PI2_B
TO_INT = 1.5 * 2.0 ** 23
TO_2_16 = 1.5 * 2.0 ** 7
SIN_SCALE = 6.283185

F32 = mybir.dt.float32
F32R = mybir.dt.float32r
U32 = mybir.dt.uint32
ALU = mybir.AluOpType
ACT = mybir.ActivationFunctionType


class Count:

    def __init__(self, sem):
        self.sem, self.at, self.n = sem, 0, 0

    def inc(self, ins):
        ins.then_inc(self.sem, 1)
        self.at = self.at + 1
        self.n += 1
        return self.at


@contextmanager
def repeat(eng, times, **per):
    start = {k: c.at for k, (c, _) in per.items()}
    seen = {k: c.n for k, (c, _) in per.items()}
    with eng.Fori(0, times) as i:
        for k, (c, m) in per.items():
            c.at = start[k] + i * m
        yield i
    for k, (c, m) in per.items():
        assert c.n - seen[k] == m, (k, c.n - seen[k], m)
        c.at, c.n = start[k] + times * m, seen[k] + times * m


def build(nc, A):
    with ExitStack() as ctx:
        def sb(name, shape, dt=F32, where=ctx):
            return where.enter_context(nc.sbuf_tensor(name, shape, dt))

        def sem(name):
            return ctx.enter_context(nc.semaphore(name))

        xs_hi = sb("xs_hi", [P, KT, SEQ], F32R)
        xs_lo = sb("xs_lo", [P, KT, SEQ], F32R)
        w_raw = [sb(f"w_raw{s}", [P, D]) for s in range(2)]
        w_hi = [sb(f"w_hi{s}", [P, D], F32R) for s in range(2)]
        w_lo = [sb(f"w_lo{s}", [P, D], F32R) for s in range(2)]
        Y = sb("Y", [P, KT, SEQ])
        rstd = sb("rstd", [P, SEQ])
        ones = sb("ones", [P, P])
        params = sb("params_sb", [P, N_PARAMS])

        def par(name, i=0, n=1):
            if isinstance(i, int):
                return params[:, PC[name] + i:PC[name] + i + n]
            return params[:, bass.ds(i + PC[name], n)]

        mix = ExitStack()
        QKV = sb("QKV", [P, KT, SEQ], where=mix)
        consts = sb("consts_sb", [P, N_CONSTS], where=mix)
        causal = sb("causal_sb", [P, P], U32, mix)
        w_a2 = sb("w_a2_sb", [RANK, SEQ], where=mix)
        g_lr = sb("g_lr", [RANK, SEQ], where=mix)
        ident = consts[:, CC["ident"]:CC["ident"] + P]
        s5 = ExitStack()
        iota_t = sb("iota_t", [P, SEQ], where=s5)
        BT = [sb(f"BT{c}", [P, S5_TILES, P], where=s5) for c in range(2)]
        CM = sb("CM", [P, 2, PAIRS, 32], where=s5)
        s5s = sb("s5s", [P, 17, PAIRS], where=s5)
        turns = sb("turns", [P, SEQ], where=s5)
        prod = sb("prod", [P, SEQ], where=s5)
        st_re = sb("st_re", [P, SEQ], where=s5)
        st_im = sb("st_im", [P, SEQ], where=s5)
        st_t = sb("st_t", [P, SEQ], where=s5)
        s5.close()
        gla = ExitStack()
        log_a = sb("log_a", [P, SEQ], where=gla)
        e_buf = sb("e_buf", [P, SEQ], where=gla)
        k_dec = sb("k_dec", [P, SEQ], where=gla)
        k_tok = sb("k_tok", [P, 4, P], where=gla)
        v_tok = sb("v_tok", [P, 4, DV], where=gla)
        sc = sb("sc", [P, 4, P], where=gla)
        S = sb("S", [P, CHUNKS - 1, DV], where=gla)
        decay = sb("decay", [P, CHUNKS], where=gla)
        gla.close()
        mix.close()
        outp = ExitStack()
        x_res = sb("x_res", [P, KT, SEQ], where=outp)
        outp.close()
        pg = ExitStack()
        p_hi = sb("p_hi", [P, PLE_KT, SEQ], F32R, pg)
        p_lo = sb("p_lo", [P, PLE_KT, SEQ], F32R, pg)
        ple = sb("ple", [P, KT, SEQ], where=pg)
        pg.close()
        mid_hi = sb("mid_hi", [P, QT, SEQ], F32R)
        mid_lo = sb("mid_lo", [P, QT, SEQ], F32R)
        conv_in = sb("conv_in", [P, SEQ + 2])
        conv_acc = sb("conv_acc", [P, SEQ])
        silu_g = sb("silu_g", [P, SEQ])
        val = sb("val", [P, SEQ])
        sq = sb("sq", [P, SEQ])
        ss = sb("ss", [P, SEQ])
        p_raw = sb("p_raw", [P, PLE_KT, SEQ])

        cos_t = [Y[:, 8 + b, :] for b in range(2)]
        sin_t = [Y[:, 10 + b, :] for b in range(2)]
        v_re = [Y[:, 12 + b, :] for b in range(2)]
        v_im = [Y[:, 14 + b, :] for b in range(2)]
        B_in = [QKV[:, 8 + c, :] for c in range(2)]
        B_bar = [QKV[:, 10 + c, :] for c in range(2)]
        B_prod = QKV[:, 12, :]
        x_sq = [QKV[:, 14 + b, :] for b in range(2)]
        x_ss = QKV[:, 7, :]
        x_var = QKV[:, 6, :]
        glu_gate = [Y[:, 9, :], Y[:, 10, :], Y[:, 11, :], Y[:, 15, :]]
        window = [Y[:, 12, :], Y[:, 13, :]]
        w_pool = Y[:, 14, :]

        bank = [ctx.enter_context(nc.psum_tensor(f"bank{b}", [P, SEQ], F32)) for b in range(8)]

        params_in = sem("params_in")
        x_in = [sem(f"x_in{g}") for g in range(4)]
        sq_used = sem("sq_used")
        s5_in = sem("s5_in")
        wpool_in = sem("wpool_in")
        a2_in = sem("a2_in")
        glu_in = sem("glu_in")
        xres_in = [sem(f"xres_in{g}") for g in range(4)]
        p_in = sem("p_in")
        w_in = [sem(f"w_landed{s}") for s in range(2)]
        hi_made = sem("hi_made")
        lo_made = sem("lo_made")
        tile_done = sem("tile_done")
        evacuated = sem("evacuated")
        xs_hi_made = sem("xs_hi_made")
        xs_lo_made = sem("xs_lo_made")
        ones_set = sem("ones_set")
        squared = sem("squared")
        sum_spread = sem("sum_spread")
        var_made = sem("var_made")
        root_made = sem("root_made")
        rstd_made = sem("rstd_made")
        dt_made = sem("dt_made")
        exp_in = sem("exp_in")
        step_trig = sem("step_trig")
        bbar_made = sem("bbar_made")
        b_turned = sem("b_turned")
        bt_made = sem("bt_made")
        cm_made = sem("cm_made")
        trig_made = sem("trig_made")
        bu_made = sem("bu_made")
        rotated_in = sem("rotated_in")
        scanned = sem("scanned")
        states_made = sem("states_made")
        states_read = sem("states_read")
        y_added = sem("y_added")
        gelu_made = sem("gelu_made")
        glu_done = sem("glu_done")
        glu_sig = sem("glu_sig")
        y_s5_made = sem("y_s5_made")
        pooled = sem("pooled")
        pool_mixed = sem("pool_mixed")
        y_pool_made = sem("y_pool_made")
        logits_made = sem("logits_made")
        logits_out = sem("logits_out")
        soft_made = sem("soft_made")
        g_made = sem("g_made")
        b_made = sem("b_made")
        eb_made = sem("eb_made")
        ebn_made = sem("ebn_made")
        qd_made = sem("qd_made")
        kd_made = sem("kd_made")
        diff_made = sem("diff_made")
        ebr_made = sem("ebr_made")
        kr_made = sem("kr_made")
        v_turned = sem("v_turned")
        v_tok_made = sem("v_tok_made")
        k_turned = sem("k_turned")
        k_tok_made = sem("k_tok_made")
        scores_made = sem("scores_made")
        sc_masked = sem("sc_masked")
        kv_made = sem("kv_made")
        S_made = sem("S_made")
        o_made = sem("o_made")
        o_out = sem("o_out")
        o_squared = sem("o_squared")
        o_summed = sem("o_summed")
        o_var = sem("o_var")
        o_root = sem("o_root")
        o_norm = sem("o_norm")
        r_silu = sem("r_silu")
        y_gla_made = sem("y_gla_made")
        sc_zeroed = sem("sc_zeroed")
        conv_made = sem("conv_made")
        silu_made = sem("silu_made")
        mid_made = sem("mid_made")
        mid_hi_made = sem("mid_hi_made")
        mid_lo_made = sem("mid_lo_made")
        p_hi_made = sem("p_hi_made")
        p_lo_made = sem("p_lo_made")
        ple_done = sem("ple_done")
        ple_out = sem("ple_out")
        gate_made = sem("gate_made")
        out_made = sem("out_made")
        written = sem("written")
        v_link = sem("vector_link")
        a_link = sem("scalar_link")
        p_link = sem("gpsimd_link")

        h_made = sem("h_made")
        step_turns = sem("step_turns")
        turns_made = sem("turns_made")

        W_FULL, W_G, W_DOWN = D, KT * RANK, QT * P
        HALF_Q = PER_QUARTER // 2

        def landed(eng, c, e=0):
            eng.wait_ge(w_in[c % 2], (e + c // 2 + 1) * 16)

        def in_width(n):
            return W_G if n == N_G else W_FULL

        def in_bank(n):
            return n if n < 4 else n % 2

        def kv_place(c):
            return bank[(3, 4, 6, 2)[2 * (c % 2) + c // 4]][:, (c // 2 % 2) * DV:(c // 2 % 2 + 1) * DV]

        block = ctx.enter_context(nc.Block())

        @block.sync
        def _(sp):
            def weights(c, e, src, width, free=True):
                if free:
                    sp.wait_ge(lo_made, 2 * e + c - 1)
                sp.dma_start(w_raw[c % 2][:, 0:width], src).then_inc(w_in[c % 2], 16)

            for n in range(IN_TILES):
                src = A["w_in_g"] if n == N_G else A["w_in"][n - (n > N_G)]
                if n == 0:
                    for g in range(4):
                        sp.dma_start(Y[:, 4 * g:4 * g + 4, :], A["x"][:, 4 * g:4 * g + 4, :]).then_inc(x_in[g], 16)
                        if g == 0:
                            sp.dma_start(params[:], A["params"]).then_inc(params_in, 16)
                            weights(n, 0, src, D, free=False)
                else:
                    weights(n, 0, src, in_width(n), free=n >= 2)
                if n == 1:
                    sp.dma_start(consts[:], A["consts"]).then_inc(s5_in, 16)
                    sp.dma_start(iota_t[:], A["iota"]).then_inc(s5_in, 16)
                    for c in range(2):
                        sp.dma_start(B_in[c], A["s5_b"][:, c, :]).then_inc(s5_in, 16)
                    sp.dma_start(CM[:], A["s5_c"]).then_inc(s5_in, 16)
                    sp.dma_start(causal[:], A["causal"]).then_inc(a2_in, 16)
                    sp.dma_start(w_a2[:], A["w_a2"]).then_inc(a2_in, 16)
                if n == HEAD_SLOT + 2:
                    sp.wait_ge(states_made, PAIRS)
                    sp.dma_start(Y[:, 12:16, :], A["w_glu"]).then_inc(glu_in, 16)
                if n == HEAD_SLOT + 5:
                    sp.wait_ge(glu_done, 4)
                    sp.dma_start(w_pool, A["w_pool"]).then_inc(wpool_in, 16)
            for s in range(2):
                weights(OUT0 + s, 0, A["w_out"][s], W_FULL)
            sp.wait_ge(y_gla_made, 2 * HEADS)
            for g in range(4):
                sp.dma_start(x_res[:, 4 * g:4 * g + 4, :], A["x"][:, 4 * g:4 * g + 4, :]).then_inc(xres_in[g], 16)
            with sp.Fori(1, KT // 2) as i:
                for s in range(2):
                    weights(OUT0 + s, i, A["w_out"][2 * i + s], W_FULL)
            with sp.Fori(0, QUARTERS) as q:
                with sp.Fori(0, QT) as i:
                    for s in range(2):
                        weights(FFN0 + s, q * HALF_Q + i, A["w_up"][q * UP + 2 * i + s], W_FULL)
                with sp.Fori(0, KT // 2) as i:
                    for s in range(2):
                        weights(FFN0 + UP + s, q * HALF_Q + i, A["w_down"][q * KT + 2 * i + s], W_DOWN)
            sp.dma_start(p_raw[:], A["p"]).then_inc(p_in, 16)
            for s in range(2):
                weights(PLE0 + s, 0, A["w_ple"][s], W_FULL)
            with sp.Fori(0, KT // 2) as i:
                for s in range(2):
                    weights(PG0 + s, i, A["w_pg"][2 * i + s], W_FULL)
            for j in range(KT):
                sp.wait_ge(out_made, j + 1)
                sp.dma_start(A["out"][:, j, :], Y[:, j, :]).then_inc(written, 16)
            sp.wait_ge(written, 16 * KT)

        @block.tensor
        def _(pe):
            def product(out, w_h, w_l, x_h, x_l, first, last):
                nc.tensor.matmul(out, w_h, x_h, start=first, stop=False)
                nc.tensor.matmul(out, w_h, x_l, start=False, stop=False)
                return nc.tensor.matmul(out, w_l, x_h, start=False, stop=last)

            def tile(slot, out, x_h, x_l, kts, before=None, m=P):
                for k in range(kts):
                    if before is not None:
                        before(k)
                    ks = slice(k * m, (k + 1) * m)
                    last = product(out, w_hi[slot][:, ks], w_lo[slot][:, ks], x_h[:, k, :], x_l[:, k, :],
                                   k == 0, k == kts - 1)
                last.then_inc(tile_done, 1)

            def spread_sum(n_squares, src, out):
                pe.wait_ge(sq_used, n_squares)
                nc.tensor.matmul(out[:], ones[:], src, start=True, stop=True).then_inc(sum_spread, 1)

            def turn_b():
                pe.wait_ge(bbar_made, 1)
                for c in range(2):
                    for j in range(S5_TILES):
                        js = slice(j * P, (j + 1) * P)
                        t = nc.tensor.transpose(bank[4 + c][:, js], B_bar[c][:, js], ident)
                t.then_inc(b_turned, 1)

            def bu(i):
                c, rows = i // 4, slice(32 * (i % 4), 32 * (i % 4) + 32)
                pe.wait_ge(bt_made, 2)
                pe.wait_ge(evacuated, 4)
                if i >= 2:
                    pe.wait_ge(rotated_in, i - 1)
                for b in range(2):
                    m = nc.tensor.matmul(bank[2 + 2 * (i % 2) + b][:], BT[b][rows, c, :], Y[rows, c, :],
                                         start=True, stop=True)
                m.then_inc(bu_made, 1)

            def read_states(i):
                c, j = i // 4, i % 4
                pe.wait_ge(cm_made, 1)
                pe.wait_ge(states_made, i + 1)
                if c >= 2:
                    pe.wait_ge(y_added, c - 1)
                if i == 4:
                    pe.wait_ge(rstd_made, 1)
                out = bank[6 + c % 2][32 * j:32 * j + 32, :]
                nc.tensor.matmul(out, CM[:, 0, i, :], st_re[:], start=True, stop=False, skip_group_check=True)
                nc.tensor.matmul(out, CM[:, 1, i, :], st_im[:], start=False, stop=True,
                                 skip_group_check=True).then_inc(states_read, 1)

            def glu(j):
                if j == 0:
                    pe.wait_ge(gelu_made, S5_TILES)
                    pe.wait_ge(glu_in, 16)
                if j == 1:
                    pe.wait_ge(logits_out, 1)
                if j == 2:
                    pe.wait_ge(sc_masked, 1)
                if j == 3:
                    pe.wait_ge(glu_sig, 3)
                for k in range(S5_TILES):
                    m = nc.tensor.matmul(bank[(6, 7, 5, 5)[j]][:], Y[:, 12 + k, j * P:(j + 1) * P], Y[:, k, :],
                                         start=k == 0, stop=k == S5_TILES - 1)
                m.then_inc(glu_done, 1)

            def mix_pool(g):
                pe.wait_ge(pooled, g + 1)
                if g == 0:
                    pe.wait_ge(wpool_in, 16)
                if g % 2:
                    pe.wait_ge(y_pool_made, g)
                else:
                    pe.wait_ge(sc_masked, g // 2 + 2)
                nc.tensor.matmul(bank[5][:], w_pool[:, g * P:(g + 1) * P], Y[:, 4 + g, :], start=True,
                                 stop=True).then_inc(pool_mixed, 1)

            def head_logits(h):
                if h == 0:
                    pe.wait_ge(a2_in, 32)
                    pe.wait_ge(y_added, 4)
                if h == 1:
                    pe.wait_ge(glu_sig, 2)
                if h >= 2:
                    pe.wait_ge(o_out, h - 1)
                nc.tensor.matmul(bank[7][:], w_a2[:, h * P:(h + 1) * P], g_lr[:], start=True,
                                 stop=True).then_inc(logits_made, 1)

            def head_turn(h):
                if h == 0:
                    pe.wait_ge(rotated_in, PAIRS)
                    pe.wait_ge(evacuated, N_V + 8)
                else:
                    pe.wait_ge(S_made, h)
                for e in range(2):
                    for j in range(4):
                        js = slice(j * P, (j + 1) * P)
                        m = nc.tensor.transpose(bank[3 + e][:, js], QKV[:, 8 + 2 * h + e, js], ident)
                m.then_inc(v_turned, 1)
                pe.wait_ge(kr_made, h + 1)
                if h >= 2:
                    pe.wait_ge(o_norm, h - 1)
                for j in range(4):
                    js = slice(j * P, (j + 1) * P)
                    m = nc.tensor.transpose(bank[2][:, js], QKV[:, 4 + h, js], ident)
                m.then_inc(k_turned, 1)
                if h == 1:
                    pe.wait_ge(glu_sig, 4)
                if h >= 2:
                    pe.wait_ge(y_pool_made, 2 * h - 2)
                for j in range(4):
                    ts = slice(j * P, (j + 1) * P)
                    m = nc.tensor.matmul(bank[5][:, ts], k_dec[:, ts], QKV[:, h, ts], start=True, stop=True)
                m.then_inc(scores_made, 1)

            def head_kv(h):
                pe.wait_ge(k_tok_made, h + 1)
                pe.wait_ge(v_tok_made, h + 1)
                if h == 0:
                    pe.wait_ge(glu_sig, 1)
                else:
                    pe.wait_ge(o_out, h)
                for c in range(CHUNKS - 1):
                    rows = slice(CHUNK * (c % 2), CHUNK * (c % 2) + CHUNK)
                    m = nc.tensor.matmul(kv_place(c), k_tok[rows, c // 2, :], v_tok[rows, c // 2, :], start=True, stop=True)
                m.then_inc(kv_made, 1)

            def head_o(h):
                pe.wait_ge(sc_masked, h + 1)
                pe.wait_ge(S_made, h + 1)
                pe.wait_ge(logits_out, min(h + 2, HEADS))
                for e in range(2):
                    es = slice(e * P, (e + 1) * P)
                    for j in range(4):
                        nc.tensor.matmul(bank[6 + e][:, j * P:(j + 1) * P], v_tok[:, j, es], sc[:, j, :],
                                         start=True, stop=False, skip_group_check=True)
                        for c in (2 * j, 2 * j + 1):
                            if c >= 1:
                                ts = slice(c * CHUNK, (c + 1) * CHUNK)
                                m = nc.tensor.matmul(bank[6 + e][:, ts], S[:, c - 1, es], QKV[:, h, ts],
                                                     start=False, stop=c % 2 == 1, skip_group_check=True)
                m.then_inc(o_made, 1)

            def head_norm(h):
                pe.wait_ge(o_squared, h + 1)
                pe.wait_ge(S_made, min(h + 2, HEADS))
                for e in range(2):
                    m = nc.tensor.matmul(bank[2][:], ones[:], QKV[:, h + 4 * e, :], start=e == 0, stop=e == 1)
                m.then_inc(o_summed, 1)

            for n in range(IN_TILES):
                pe.wait_ge(lo_made, n + 1)
                if n >= 4:
                    pe.wait_ge(evacuated, n - 1)

                def before(k, n=n):
                    if n == 0:
                        pe.wait_ge(xs_lo_made, k + 1)
                    if k == KT // 2:
                        if n == HEAD_SLOT + 3:
                            glu(3)
                        if n in (HEAD_SLOT + 5, HEAD_SLOT + 7):
                            mix_pool(n - HEAD_SLOT - 4)
                        if n in (HEAD_SLOT + 5, HEAD_SLOT + 7, HEAD_SLOT + 9):
                            head_norm((n - HEAD_SLOT - 5) // 2)

                m = RANK if n == N_G else P
                tile(n % 2, bank[in_bank(n)][0:m, :], xs_hi, xs_lo, KT, before, m)
                if n == 2:
                    pe.wait_ge(ones_set, 1)
                    spread_sum(KT, x_ss, bank[7])
                if n == 3:
                    turn_b()
                if READ_SLOT <= n < READ_SLOT + PAIRS:
                    read_states(n - READ_SLOT)
                if BU_SLOT <= n < BU_SLOT + PAIRS:
                    bu(n - BU_SLOT)
                s = n - HEAD_SLOT
                if s >= 3 and s % 2 == 1:
                    head_o((s - 3) // 2)
                if s in (0, 2, 4, 6):
                    head_logits(s // 2)
                if s in (1, 3, 5, 7):
                    head_turn((s - 1) // 2)
                if s in (2, 4, 6, 8):
                    head_kv((s - 2) // 2)
                if s == 1:
                    glu(0)
                    glu(1)
                if s == 2:
                    glu(2)
                if s in (4, 6):
                    mix_pool(s - 4)

            for n in (OUT0, OUT0 + 1):
                pe.wait_ge(lo_made, n + 1)
                pe.wait_ge(evacuated, n - 1)

                def before(k, n=n):
                    if n == OUT0:
                        pe.wait_ge(xs_lo_made, KT + k + 1)
                        if k == 2:
                            head_norm(HEADS - 1)

                tile(n % 2, bank[n % 2][:], xs_hi, xs_lo, KT, before)
            with pe.Fori(1, KT // 2) as i:
                for s in range(2):
                    pe.wait_ge(lo_made, 2 * i + (OUT0 + s + 1))
                    pe.wait_ge(evacuated, 2 * i + (OUT0 + s - 1))
                    tile((OUT0 + s) % 2, bank[(OUT0 + s) % 2][:], xs_hi, xs_lo, KT)

            spread_sum(2 * KT, ss[:], bank[2])
            with pe.Fori(0, QUARTERS) as q:
                with pe.Fori(0, QT) as i:
                    for s in range(2):
                        n = PER_QUARTER * q + 2 * i + (FFN0 + s)
                        pe.wait_ge(lo_made, n + 1)
                        pe.wait_ge(evacuated, n - 1)
                        before = (lambda k: pe.wait_ge(xs_lo_made, 2 * KT + k + 1)) if s == 0 else None
                        tile((FFN0 + s) % 2, bank[(FFN0 + s) % 2][:], xs_hi, xs_lo, KT, before)
                with pe.Fori(0, KT // 2) as i:
                    for s in range(2):
                        n = PER_QUARTER * q + 2 * i + (FFN0 + UP + s)
                        pe.wait_ge(lo_made, n + 1)
                        pe.wait_ge(evacuated, n - 1)

                        def before(k, s=s, q=q):
                            if s == 0 and k in (0, QT - 1):
                                pe.wait_ge(mid_lo_made, QT * q + (QT - 1 if k == 0 else QT))

                        tile((FFN0 + UP + s) % 2, bank[(FFN0 + UP + s) % 2][:], mid_hi, mid_lo, QT, before)

            pe.wait_ge(p_lo_made, PLE_KT)
            for s in range(2):
                pe.wait_ge(lo_made, PLE0 + s + 1)
                slot = (PLE0 + s) % 2
                for u in range(PLE_PER):
                    j = PLE_PER * s + u
                    if j >= 4:
                        pe.wait_ge(ple_out, j - 3)
                    for k in range(PLE_KT):
                        ks = slice((u * PLE_KT + k) * P, (u * PLE_KT + k + 1) * P)
                        m = product(bank[3 + j % 4][:], w_hi[slot][:, ks], w_lo[slot][:, ks], p_hi[:, k, :],
                                    p_lo[:, k, :], k == 0, k == PLE_KT - 1)
                    m.then_inc(ple_done, 1)
            spread_sum((2 + QUARTERS) * KT, ss[:], bank[2])
            with pe.Fori(0, KT // 2) as i:
                for s in range(2):
                    pe.wait_ge(lo_made, 2 * i + (PG0 + s + 1))
                    pe.wait_ge(evacuated, 2 * i + (PG0 - 2 + s - 1))
                    before = (lambda k: pe.wait_ge(xs_lo_made, 3 * KT + k + 1)) if s == 0 else None
                    tile((PG0 + s) % 2, bank[(PG0 + s) % 2][:], xs_hi, xs_lo, KT, before)
            spread_sum((3 + QUARTERS) * KT, ss[:], bank[2])

        @block.scalar
        def _(act):
            link_count = Count(a_link)

            def link(ins):
                act.wait_ge(a_link, link_count.inc(ins))

            def w_half(c, e=0, width=W_FULL, used=0):
                landed(act, c, e)
                act.wait_ge(tile_done, 2 * e + (c - 1 - used))
                nc.scalar.activation(w_hi[c % 2][:, 0:width], w_raw[c % 2][:, 0:width], ACT.Copy).then_inc(hi_made, 1)

            def w_first(c):
                landed(act, c)
                nc.scalar.activation(w_hi[c % 2][:], w_raw[c % 2][:], ACT.Copy).then_inc(hi_made, 1)

            def x_half(k, gain=None):
                scale = 1.0 if gain is None else par(gain, k)
                nc.scalar.activation(xs_hi[:, k, :], Y[:, k, :], ACT.Identity, scale=scale).then_inc(xs_hi_made, 1)

            def square(src, used, made):
                act.wait_ge(evacuated, made)
                act.wait_ge(sq_used, used)
                nc.scalar.activation(sq[:], src, ACT.Square).then_inc(squared, 1)

            def root(n, src):
                act.wait_ge(var_made, n + 1)
                nc.scalar.activation(rstd[:], src, ACT.Sqrt).then_inc(root_made, 1)

            def trig(i):
                act.wait_ge(turns_made, i + 1)
                if i < 2:
                    act.wait_ge(tile_done, 1)
                else:
                    act.wait_ge(states_made, i - 1)
                nc.scalar.activation(sin_t[i % 2], turns[:], ACT.Sin, scale=SIN_SCALE)
                link(nc.scalar.activation(cos_t[i % 2], turns[:], ACT.Sin, scale=math.pi))
                nc.scalar.activation(cos_t[i % 2], cos_t[i % 2], ACT.Square).then_inc(trig_made, 1)

            def head_gate(h):
                act.wait_ge(logits_made, h + 1)
                if h >= 1:
                    act.wait_ge(kr_made, h)
                nc.scalar.activation(log_a[:], bank[7][:], ACT.Identity, bias=par("b_a", h)).then_inc(logits_out, 1)
                act.wait_ge(logits_out, h + 1)
                link(nc.scalar.activation(e_buf[:], log_a[:], ACT.Abs))
                link(nc.scalar.activation(e_buf[:], e_buf[:], ACT.Exp, scale=-1.0))
                nc.scalar.activation(e_buf[:], e_buf[:], ACT.Ln, bias=1.0).then_inc(soft_made, 1)
                act.wait_ge(b_made, h + 1)
                nc.scalar.activation(decay[:], log_a[:, CHUNK - 1:SEQ:CHUNK], ACT.Exp, scale=1 / 16)
                nc.scalar.activation(e_buf[:], log_a[:], ACT.Exp, scale=1 / 16).then_inc(eb_made, 1)
                act.wait_ge(qd_made, h + 1)
                nc.scalar.activation(e_buf[:], log_a[:], ACT.Exp, scale=-1 / 16).then_inc(ebn_made, 1)
                act.wait_ge(diff_made, h + 1)
                nc.scalar.activation(e_buf[:], e_buf[:], ACT.Exp, scale=1 / 16).then_inc(ebr_made, 1)

            def head_tokens(h):
                act.wait_ge(v_turned, h + 1)
                for e in range(2):
                    m = nc.scalar.activation(v_tok[:, :, e * P:(e + 1) * P],
                                             bank[3 + e][:].rearrange("p (j d) -> p j d", j=4), ACT.Copy)
                m.then_inc(v_tok_made, 1)
                act.wait_ge(k_turned, h + 1)
                nc.scalar.activation(k_tok[:], bank[2][:].rearrange("p (j d) -> p j d", j=4),
                                     ACT.Copy).then_inc(k_tok_made, 1)

            def head_out(h):
                act.wait_ge(o_made, h + 1)
                for e in range(2):
                    m = nc.scalar.activation(QKV[:, 8 + 2 * h + e, :], bank[6 + e][:], ACT.Copy)
                m.then_inc(o_out, 1)
                act.wait_ge(o_out, h + 1)
                for e in range(2):
                    m = nc.scalar.activation(QKV[:, h + 4 * e, :], QKV[:, 8 + 2 * h + e, :], ACT.Square)
                m.then_inc(o_squared, 1)

            def head_root(h):
                act.wait_ge(o_var, h + 1)
                nc.scalar.activation(QKV[:, 4 + h, :], QKV[:, h, :], ACT.Sqrt).then_inc(o_root, 1)

            def gate_glu(j):
                act.wait_ge(glu_done, j + 1)
                nc.scalar.activation(glu_gate[j], bank[(6, 7, 5, 5)[j]][:], ACT.Sigmoid,
                                     bias=par("b_glu", j)).then_inc(glu_sig, 1)

            def silu_r(k):
                act.wait_ge(evacuated, N_R + k + 1)
                nc.scalar.activation(Y[:, 8 + k, :], Y[:, 8 + k, :], ACT.Silu).then_inc(r_silu, 1)

            act.wait_ge(params_in, 16)
            for g in range(4):
                act.wait_ge(x_in[g], 16)
                for k in range(4 * g, 4 * g + 4):
                    x_half(k, "mix")
                if g == 0:
                    w_first(0)
            w_first(1)
            for k in range(KT):
                if k >= 2:
                    act.wait_ge(sq_used, k - 1)
                nc.scalar.activation(x_sq[k % 2], Y[:, k, :], ACT.Square).then_inc(squared, 1)
                if k == KT // 2 - 1:
                    w_half(2)
            nc.scalar.activation(s5s[:, 0, :], par("log_dt", 0, PAIRS), ACT.Exp).then_inc(dt_made, 1)
            act.wait_ge(exp_in, 1)
            nc.scalar.activation(s5s[:, 3, :], s5s[:, 1, :], ACT.Exp)
            act.wait_ge(step_turns, 1)
            nc.scalar.activation(s5s[:, 9, :], s5s[:, 6, :], ACT.Sin, scale=SIN_SCALE)
            nc.scalar.activation(s5s[:, 10, :], s5s[:, 6, :], ACT.Sin, scale=math.pi).then_inc(step_trig, 1)
            w_half(3)
            root(0, x_var)
            for n in range(2, IN_TILES):
                s = n - HEAD_SLOT
                if s == 3:
                    gate_glu(3)
                if s in (5, 7, 9):
                    head_root((s - 5) // 2)
                w_half(n + 2, width=in_width(n + 2))
                if n == 3:
                    act.wait_ge(b_turned, 1)
                    for c in range(2):
                        nc.scalar.activation(BT[c][:], bank[4 + c][:].rearrange("p (j d) -> p j d", j=4),
                                             ACT.Copy).then_inc(bt_made, 1)
                if BU_SLOT - 1 <= n < BU_SLOT - 1 + PAIRS:
                    trig(n - BU_SLOT + 1)
                if s == 0:
                    for c in range(S5_TILES):
                        act.wait_ge(y_added, c + 1)
                        nc.scalar.activation(Y[:, c, :], Y[:, c, :], ACT.Gelu_apprx_tanh).then_inc(gelu_made, 1)
                if s >= 3 and s % 2 == 1:
                    head_out((s - 3) // 2)
                if s in (0, 2, 4, 6):
                    head_gate(s // 2)
                if s in (1, 3, 5, 7):
                    head_tokens((s - 1) // 2)
                if s in (1, 2):
                    for j in ((0, 1), (2,))[s - 1]:
                        gate_glu(j)
                if s in (5, 7, 9):
                    silu_r(s - 5)
                    silu_r(s - 4)
            act.wait_ge(tile_done, IN_TILES)
            for k in range(KT):
                if k == 4:
                    head_root(HEADS - 1)
                    silu_r(6)
                    silu_r(7)
                if k < 4:
                    act.wait_ge(y_s5_made, 4)
                elif k < 8:
                    act.wait_ge(y_pool_made, 4)
                else:
                    act.wait_ge(y_gla_made, k - 7)
                x_half(k)
            with act.Fori(0, KT // 2 - 1) as i:
                for s in range(2):
                    w_half(OUT0 + 2 + s, i)
                    square(Y[:, bass.ds(2 * i + s, 1), :], 2 * i + (KT + s), 2 * i + (OUT0 + s + 1))
            w_half(FFN0)
            square(Y[:, KT - 2, :], 2 * KT - 2, FFN0 - 1)
            square(Y[:, KT - 1, :], 2 * KT - 1, FFN0)
            for k in range(KT):
                x_half(k, "ffn")
                if k == KT // 2 - 1:
                    w_half(FFN0 + 1)
            root(1, val[:])

            def up_pair(q, i, width):
                e = q * HALF_Q + i
                f = q * QT + i
                w_half(FFN0 + 2, e, width)
                act.wait_ge(conv_made, f + 1)
                nc.scalar.activation(silu_g[:], conv_acc[:], ACT.Silu).then_inc(silu_made, 1)
                act.wait_ge(mid_made, f + 1)
                dst = mid_hi[:, i, :] if isinstance(i, int) else mid_hi[:, bass.ds(i, 1), :]
                nc.scalar.activation(dst, val[:], ACT.Copy).then_inc(mid_hi_made, 1)
                w_half(FFN0 + 3, e, width)

            with act.Fori(0, QUARTERS) as q:
                with act.Fori(0, QT - 1) as i:
                    up_pair(q, i, W_FULL)
                up_pair(q, QT - 1, W_DOWN)
                with act.Fori(0, KT // 2 - 1) as i:
                    for s in range(2):
                        w_half(FFN0 + UP + 2 + s, q * HALF_Q + i, W_DOWN)
                        square(Y[:, bass.ds(2 * i + s, 1), :], KT * q + 2 * i + (2 * KT + s),
                               PER_QUARTER * q + 2 * i + (FFN0 + UP + s + 1))
                for s in range(2):
                    w_half(FFN0 + PER_QUARTER + s, q * HALF_Q)
                    square(Y[:, KT - 2 + s, :], KT * q + (3 * KT - 2 + s), PER_QUARTER * q + (FFN0 + PER_QUARTER - 1 + s))

            act.wait_ge(p_in, 16)
            act.wait_ge(tile_done, PLE0)
            for k in range(PLE_KT):
                nc.scalar.activation(p_hi[:, k, :], p_raw[:, k, :], ACT.Copy).then_inc(p_hi_made, 1)
            for k in range(KT):
                x_half(k, "ple")
                if k == 10:
                    landed(act, PG0)
                    act.wait_ge(ple_done, PLE_PER)
                    nc.scalar.activation(w_hi[PG0 % 2][:], w_raw[PG0 % 2][:], ACT.Copy).then_inc(hi_made, 1)
                act.wait_ge(ple_done, k + 1)
                nc.scalar.activation(ple[:, k, :], bank[3 + k % 4][:], ACT.Copy).then_inc(ple_out, 1)
            w_first(PG0 + 1)
            root(2, val[:])

            def gate(i, s, last):
                j = 2 * i + s
                if not last:
                    w_half(PG0 + 2 + s, i, used=2)
                act.wait_ge(evacuated, j + (PG0 - 2 + 1))
                nc.scalar.activation(conv_acc[:], conv_acc[:], ACT.Sigmoid).then_inc(gate_made, 1)
                act.wait_ge(h_made, j + 1)
                act.wait_ge(sq_used, j + (2 + QUARTERS) * KT)
                src = Y[:, j, :] if isinstance(i, int) else Y[:, bass.ds(j, 1), :]
                nc.scalar.activation(sq[:], src, ACT.Square).then_inc(squared, 1)

            with act.Fori(0, KT // 2 - 1) as i:
                for s in range(2):
                    gate(i, s, False)
            for s in range(2):
                gate(KT // 2 - 1, s, True)
            root(3, val[:])

        @block.vector
        def _(dve):
            tt, ts, stt = nc.vector.tensor_tensor, nc.vector.tensor_scalar, nc.vector.scalar_tensor_tensor
            links = Count(v_link)

            def link(ins):
                dve.wait_ge(v_link, links.inc(ins))

            def w_rest(c, e=0, width=W_FULL):
                dve.wait_ge(hi_made, 2 * e + (c + 1))
                tt(w_lo[c % 2][:, 0:width], w_raw[c % 2][:, 0:width], w_hi[c % 2][:, 0:width].bitcast(F32),
                   ALU.subtract).then_inc(lo_made, 1)

            def x_rest(k, stage, gain=None):
                dve.wait_ge(xs_hi_made, stage * KT + k + 1)
                hi = xs_hi[:, k, :].bitcast(F32)
                if gain is None:
                    ins = tt(xs_lo[:, k, :], Y[:, k, :], hi, ALU.subtract)
                else:
                    ins = stt(xs_lo[:, k, :], Y[:, k, :], par(gain, k), hi, ALU.mult, ALU.subtract)
                ins.then_inc(xs_lo_made, 1)

            def add_square(n):
                dve.wait_ge(squared, n + 1)
                tt(ss[:], ss[:], sq[:], ALU.add).then_inc(sq_used, 1)
                dve.wait_ge(sq_used, n + 1)

            def newton(y, v, t):
                link(nc.vector.reciprocal(y, y))
                link(tt(t, y, y, ALU.mult))
                link(tt(t, t, v, ALU.mult))
                link(ts(t, t, -0.5, 1.5, ALU.mult, ALU.add))
                return tt(y, y, t, ALU.mult)

            def rms(n, spread, v):
                dve.wait_ge(sum_spread, n + 1)
                ts(v, spread[:], 1.0 / D, EPS, ALU.mult, ALU.add).then_inc(var_made, 1)
                dve.wait_ge(root_made, n + 1)
                newton(rstd[:], v, spread[:]).then_inc(rstd_made, 1)
                dve.wait_ge(rstd_made, n + 1)

            def evacuate(n):
                dve.wait_ge(tile_done, n + 1)
                m = RANK if n == N_G else P
                if n < N_Q:
                    dst = Y[:, n, :]
                elif n < N_G:
                    dst = QKV[:, n - N_Q, :]
                elif n == N_G:
                    dst = g_lr[:]
                elif n < N_POOL:
                    dst = QKV[:, 8 + n - N_V, :]
                elif n < N_R:
                    dst = Y[:, 4 + n - N_POOL, :]
                else:
                    if n == N_R + 4:
                        dve.wait_ge(pooled, POOL_TILES)
                    if n == N_R + 6:
                        dve.wait_ge(pool_mixed, POOL_TILES)
                    dst = Y[:, 8 + n - N_R, :]
                tt(dst, bank[in_bank(n)][0:m, :], rstd[0:m, :], ALU.mult).then_inc(evacuated, 1)

            def s5_constants():
                a_re, a_im = par("a_re", 0, PAIRS), par("a_im", 0, PAIRS)
                c = [s5s[:, k, :] for k in range(17)]
                dve.wait_ge(dt_made, 1)
                tt(c[1], a_re, c[0], ALU.mult).then_inc(exp_in, 1)
                link(tt(c[2], a_im, c[0], ALU.mult))
                link(ts(c[4], c[2], INV_2PI, TO_INT, ALU.mult, ALU.add))
                link(ts(c[4], c[4], TO_INT, None, ALU.subtract))
                link(stt(c[5], c[4], -PI2_A, c[2], ALU.mult, ALU.add))
                link(stt(c[5], c[4], -PI2_B, c[5], ALU.mult, ALU.add))
                link(stt(c[5], c[4], -PI2_C, c[5], ALU.mult, ALU.add))
                link(ts(c[6], c[5], INV_2PI, 0.5, ALU.mult, ALU.min))
                ts(c[6], c[6], -0.5, None, ALU.max).then_inc(step_turns, 1)
                dve.wait_ge(step_turns, 1)
                link(ts(c[7], c[6], TO_2_16, None, ALU.add))
                link(ts(c[7], c[7], TO_2_16, None, ALU.subtract))
                link(tt(c[8], c[6], c[7], ALU.subtract))
                dve.wait_ge(step_trig, 1)
                link(tt(c[10], c[10], c[10], ALU.mult))
                link(ts(c[10], c[10], -2.0, 1.0, ALU.mult, ALU.add))
                link(tt(c[11], c[3], c[10], ALU.mult))
                link(tt(c[12], c[3], c[9], ALU.mult))
                link(ts(c[11], c[11], -1.0, None, ALU.add))
                link(tt(c[13], a_re, a_re, ALU.mult))
                link(tt(c[14], a_im, a_im, ALU.mult))
                link(tt(c[13], c[13], c[14], ALU.add))
                link(nc.vector.reciprocal(c[13], c[13]))
                link(tt(c[14], c[11], a_re, ALU.mult))
                link(tt(c[15], c[12], a_im, ALU.mult))
                link(tt(c[14], c[14], c[15], ALU.add))
                link(tt(c[14], c[14], c[13], ALU.mult))
                link(tt(c[15], c[12], a_re, ALU.mult))
                link(tt(c[16], c[11], a_im, ALU.mult))
                link(tt(c[15], c[15], c[16], ALU.subtract))
                link(tt(c[15], c[15], c[13], ALU.mult))
                dve.wait_ge(s5_in, 80)

                def blocks(a):
                    return a.rearrange("p (i c) -> p i c", c=32)

                f = [c[14 + z].unsqueeze(2).to_broadcast([P, PAIRS, 32]) for z in range(2)]
                link(tt(blocks(B_bar[0]), blocks(B_in[0]), f[0], ALU.mult))
                link(tt(blocks(B_prod), blocks(B_in[1]), f[1], ALU.mult))
                link(tt(B_bar[0], B_bar[0], B_prod, ALU.subtract))
                link(tt(blocks(B_bar[1]), blocks(B_in[1]), f[0], ALU.mult))
                link(tt(blocks(B_prod), blocks(B_in[0]), f[1], ALU.mult))
                tt(B_bar[1], B_bar[1], B_prod, ALU.add).then_inc(bbar_made, 1)
                ts(CM[:, 1, :, :], CM[:, 1, :, :], -1.0, None, ALU.mult).then_inc(cm_made, 1)

            def find_turns(i):
                col = [s5s[:, k, i:i + 1] for k in (6, 7, 8)]
                if i >= 1:
                    dve.wait_ge(trig_made, i)
                link(ts(turns[:], iota_t[:], col[0], TO_INT, ALU.mult, ALU.add))
                link(ts(turns[:], turns[:], TO_INT, None, ALU.subtract))
                link(stt(turns[:], iota_t[:], col[1], turns[:], ALU.mult, ALU.subtract))
                link(stt(turns[:], iota_t[:], col[2], turns[:], ALU.mult, ALU.add))
                ts(turns[:], turns[:], 0.5, -0.5, ALU.min, ALU.max).then_inc(turns_made, 1)

            def rotate_scan(i):
                cos, sin, re, im = cos_t[i % 2], sin_t[i % 2], v_re[i % 2], v_im[i % 2]
                b_re, b_im = bank[2 + 2 * (i % 2)][:], bank[3 + 2 * (i % 2)][:]
                size = s5s[:, 3, i:i + 1].to_broadcast([P, SEQ])
                dve.wait_ge(trig_made, i + 1)
                link(ts(cos, cos, -2.0, 1.0, ALU.mult, ALU.add))
                dve.wait_ge(bu_made, i + 1)
                tt(re, b_re, cos, ALU.mult)
                tt(im, b_im, cos, ALU.mult)
                link(tt(prod[:], b_im, sin, ALU.mult))
                link(tt(re, re, prod[:], ALU.add))
                tt(prod[:], b_re, sin, ALU.mult).then_inc(rotated_in, 1)
                dve.wait_ge(rotated_in, i + 1)
                link(tt(im, im, prod[:], ALU.subtract))
                nc.vector.tensor_tensor_scan(re, size, re, 0.0, ALU.mult, ALU.add)
                nc.vector.tensor_tensor_scan(im, size, im, 0.0, ALU.mult, ALU.add).then_inc(scanned, 1)

            def add_skip(c):
                dve.wait_ge(states_read, 4 * c + 4)
                stt(Y[:, c, :], Y[:, c, :], par("d", c), bank[6 + c % 2][:], ALU.mult, ALU.add).then_inc(y_added, 1)

            def head_gate(h):
                q, k = QKV[:, h, :], QKV[:, 4 + h, :]

                def chunks(a):
                    return a.rearrange("p (n t) -> p n t", t=CHUNK)

                dve.wait_ge(soft_made, h + 1)
                link(stt(log_a[:], log_a[:], 0.0, e_buf[:], ALU.min, ALU.subtract))
                for c in range(CHUNKS):
                    ts_ = slice(c * CHUNK, (c + 1) * CHUNK)
                    m = nc.vector.tensor_tensor_scan(log_a[:, ts_], ones[:, 0:CHUNK], log_a[:, ts_], 0.0, ALU.mult,
                                                     ALU.add)
                m.then_inc(b_made, 1)
                dve.wait_ge(eb_made, h + 1)
                stt(q, q, float(P) ** -0.5, e_buf[:], ALU.mult, ALU.mult).then_inc(qd_made, 1)
                dve.wait_ge(ebn_made, h + 1)
                tt(k_dec[:], k, e_buf[:], ALU.mult).then_inc(kd_made, 1)
                dve.wait_ge(kd_made, h + 1)
                last = log_a[:, CHUNK - 1:SEQ:CHUNK].unsqueeze(2).to_broadcast([P, CHUNKS, CHUNK])
                tt(chunks(e_buf[:]), last, chunks(log_a[:]), ALU.subtract).then_inc(diff_made, 1)
                dve.wait_ge(ebr_made, h + 1)
                tt(k, k, e_buf[:], ALU.mult).then_inc(kr_made, 1)

            def head_mask(h):
                dve.wait_ge(scores_made, h + 1)
                mask = causal[:].unsqueeze(1).to_broadcast([P, 4, P])
                nc.vector.copy_predicated(sc[:], mask, bank[5][:].rearrange("p (j t) -> p j t",
                                                                            j=4)).then_inc(sc_masked, 1)

            def head_state(h):
                dve.wait_ge(kv_made, h + 1)
                for c in range(CHUNKS - 1):
                    kv = kv_place(c)
                    if c == 0:
                        ins = nc.vector.tensor_copy(S[:, 0, :], kv)
                    else:
                        ins = stt(S[:, c, :], S[:, c - 1, :], decay[:, c:c + 1], kv, ALU.mult, ALU.add)
                    if c < CHUNKS - 2:
                        link(ins)
                ins.then_inc(S_made, 1)

            def head_rms(h):
                v, y = QKV[:, h, :], QKV[:, 4 + h, :]
                dve.wait_ge(o_summed, h + 1)
                ts(v, bank[2][:], 1.0 / DV, EPS, ALU.mult, ALU.add).then_inc(o_var, 1)
                dve.wait_ge(o_root, h + 1)
                link(newton(y, v, bank[2][:]))
                for e in range(2):
                    o = QKV[:, 8 + 2 * h + e, :]
                    m = stt(o, o, par("gla_w", e), y, ALU.mult, ALU.mult)
                m.then_inc(o_norm, 1)
                dve.wait_ge(o_norm, h + 1)

            def gate_r(k):
                dve.wait_ge(r_silu, k + 1)
                tt(Y[:, 8 + k, :], Y[:, 8 + k, :], QKV[:, 8 + k, :], ALU.mult).then_inc(y_gla_made, 1)

            def scale_pool(g):
                dve.wait_ge(pool_mixed, g + 1)
                ts(Y[:, 4 + g, :], bank[5][:], par("pscale", g), None, ALU.mult).then_inc(y_pool_made, 1)

            nc.vector.memset(ones[:], 1.0).then_inc(ones_set, 1)
            link(nc.vector.memset(x_ss, 0.0))
            for g in range(4):
                for k in range(4 * g, 4 * g + 4):
                    x_rest(k, 0, "mix")
                if g == 0:
                    w_rest(0)
            w_rest(1)
            for k in range(KT):
                dve.wait_ge(squared, k + 1)
                tt(x_ss, x_ss, x_sq[k % 2], ALU.add).then_inc(sq_used, 1)
                dve.wait_ge(sq_used, k + 1)
                if k == KT // 2 - 1:
                    w_rest(2)
            s5_constants()
            w_rest(3)
            rms(0, bank[7], x_var)
            evacuate(0)
            evacuate(1)
            for n in range(2, IN_TILES):
                s = n - HEAD_SLOT
                if s == 3:
                    dve.wait_ge(glu_sig, 4)
                    for j in range(4):
                        tt(Y[:, j, :], Y[:, j, :], glu_gate[j], ALU.mult).then_inc(y_s5_made, 1)
                    dve.wait_ge(y_s5_made, 4)
                if s in (5, 7):
                    scale_pool(s - 4)
                if s in (5, 7, 9):
                    head_rms((s - 5) // 2)
                evacuate(n)
                w_rest(n + 2, width=in_width(n + 2))
                if BU_SLOT - 1 <= n < BU_SLOT - 1 + PAIRS:
                    find_turns(n - BU_SLOT + 1)
                if BU_SLOT <= n < BU_SLOT + PAIRS:
                    rotate_scan(n - BU_SLOT)
                if READ_SLOT + 3 <= n < READ_SLOT + PAIRS and (n - READ_SLOT) % 4 == 3:
                    add_skip((n - READ_SLOT) // 4)
                if s == 0:
                    dve.wait_ge(y_added, 4)
                    nc.vector.memset(sc[:], 0.0).then_inc(sc_zeroed, 1)
                    dve.wait_ge(sc_zeroed, 1)
                if s in (2, 4, 6, 8):
                    head_state((s - 2) // 2)
                if s in (0, 2, 4, 6):
                    head_gate(s // 2)
                if s in (1, 3, 5, 7):
                    head_mask((s - 1) // 2)
                if s in (4, 6):
                    scale_pool(s - 4)
                if s in (5, 7, 9):
                    gate_r(s - 5)
                    gate_r(s - 4)
            for k in range(KT):
                if k == 4:
                    head_rms(HEADS - 1)
                    gate_r(6)
                    gate_r(7)
                x_rest(k, 1)
            link(nc.vector.memset(ss[:], 0.0))

            def add_x(i, s, follow):
                j = 2 * i + s
                dve.wait_ge(tile_done, j + (OUT0 + 1))
                row = (lambda a: a[:, j, :]) if isinstance(i, int) else (lambda a: a[:, bass.ds(j, 1), :])
                out = bank[(OUT0 + s) % 2][:] if isinstance(i, int) else bank[(OUT0 + s) % 2][:].unsqueeze(1)
                tt(row(Y), row(x_res), out, ALU.add).then_inc(evacuated, 1)
                if follow is not None:
                    w_rest(*follow)
                add_square(j + KT)

            for g in range(4):
                dve.wait_ge(xres_in[g], 16)
            with repeat(dve, KT // 2 - 1, links=(links, 0)) as i:
                for s in range(2):
                    add_x(i, s, (OUT0 + 2 + s, i))
            add_x(KT // 2 - 1, 0, (FFN0,))
            add_x(KT // 2 - 1, 1, None)
            for k in range(KT):
                x_rest(k, 2, "ffn")
                if k == KT // 2 - 1:
                    w_rest(FFN0 + 1)
            rms(1, bank[2], val[:])
            link(nc.vector.memset(conv_in[:], 0.0))

            def up_pair(q, i, width):
                e, f = q * HALF_Q + i, q * QT + i
                n = PER_QUARTER * q + 2 * i
                dve.wait_ge(tile_done, n + (FFN0 + 1))
                tt(conv_in[:, 2:], bank[FFN0 % 2][:], rstd[:], ALU.mult).then_inc(evacuated, 1)
                dve.wait_ge(evacuated, n + (FFN0 + 1))
                link(ts(conv_acc[:], conv_in[:, 2:], par("conv_w", 3 * f + 2), par("conv_b", f), ALU.mult, ALU.add))
                link(stt(conv_acc[:], conv_in[:, 1:SEQ + 1], par("conv_w", 3 * f + 1), conv_acc[:], ALU.mult, ALU.add))
                stt(conv_acc[:], conv_in[:, 0:SEQ], par("conv_w", 3 * f), conv_acc[:], ALU.mult,
                    ALU.add).then_inc(conv_made, 1)
                w_rest(FFN0 + 2, e, width)
                dve.wait_ge(conv_made, f + 1)
                dve.wait_ge(tile_done, n + (FFN0 + 2))
                tt(val[:], bank[(FFN0 + 1) % 2][:], rstd[:], ALU.mult).then_inc(evacuated, 1)
                dve.wait_ge(evacuated, n + (FFN0 + 2))
                dve.wait_ge(silu_made, f + 1)
                tt(val[:], val[:], silu_g[:], ALU.mult).then_inc(mid_made, 1)
                dve.wait_ge(mid_hi_made, f + 1)
                if isinstance(i, int):
                    hi, lo, v = mid_hi[:, i, :], mid_lo[:, i, :], val[:]
                else:
                    hi, lo = mid_hi[:, bass.ds(i, 1), :], mid_lo[:, bass.ds(i, 1), :]
                    v = val[:].unsqueeze(1)
                tt(lo, v, hi.bitcast(F32), ALU.subtract).then_inc(mid_lo_made, 1)
                dve.wait_ge(mid_lo_made, f + 1)
                w_rest(FFN0 + 3, e, width)

            def add_down(q, i, s, follow, width):
                j = 2 * i + s
                n = PER_QUARTER * q + j
                dve.wait_ge(tile_done, n + (FFN0 + UP + 1))
                out = bank[(FFN0 + UP + s) % 2][:]
                if isinstance(i, int):
                    y = Y[:, j, :]
                else:
                    y, out = Y[:, bass.ds(j, 1), :], out.unsqueeze(1)
                tt(y, y, out, ALU.add).then_inc(evacuated, 1)
                w_rest(follow, q * HALF_Q + (i if width == W_DOWN else 0), width)
                add_square(KT * q + j + 2 * KT)

            with repeat(dve, QUARTERS, links=(links, 2 * QT + 1)) as q:
                with repeat(dve, QT - 1, links=(links, 2)) as i:
                    up_pair(q, i, W_FULL)
                link(nc.vector.memset(ss[:], 0.0))
                up_pair(q, QT - 1, W_DOWN)
                with repeat(dve, KT // 2 - 1, links=(links, 0)) as i:
                    for s in range(2):
                        add_down(q, i, s, FFN0 + UP + 2 + s, W_DOWN)
                for s in range(2):
                    add_down(q, KT // 2 - 1, s, FFN0 + PER_QUARTER + s, W_FULL)

            for k in range(PLE_KT):
                dve.wait_ge(p_hi_made, k + 1)
                tt(p_lo[:, k, :], p_raw[:, k, :], p_hi[:, k, :].bitcast(F32), ALU.subtract).then_inc(p_lo_made, 1)
            for k in range(KT):
                x_rest(k, 3, "ple")
                if k == 10:
                    w_rest(PG0)
            w_rest(PG0 + 1)
            rms(2, bank[2], val[:])
            link(nc.vector.memset(ss[:], 0.0))

            def add_gated(i, s, follow):
                j = 2 * i + s
                dve.wait_ge(tile_done, j + (PG0 - 2 + 1))
                tt(conv_acc[:], bank[(PG0 + s) % 2][:], rstd[:], ALU.mult).then_inc(evacuated, 1)
                if follow is not None:
                    w_rest(*follow)
                if isinstance(i, int):
                    y, g, v, gate = Y[:, j, :], ple[:, j, :], val[:], conv_acc[:]
                else:
                    y, g = Y[:, bass.ds(j, 1), :], ple[:, bass.ds(j, 1), :]
                    v, gate = val[:].unsqueeze(1), conv_acc[:].unsqueeze(1)
                dve.wait_ge(gate_made, j + 1)
                link(tt(v, gate, g, ALU.mult))
                tt(y, y, v, ALU.add).then_inc(h_made, 1)
                dve.wait_ge(h_made, j + 1)
                add_square(j + (2 + QUARTERS) * KT)

            with repeat(dve, KT // 2 - 1, links=(links, 2)) as i:
                for s in range(2):
                    add_gated(i, s, (PG0 + 2 + s, i))
            for s in range(2):
                add_gated(KT // 2 - 1, s, None)
            rms(3, bank[2], val[:])
            for j in range(KT):
                stt(Y[:, j, :], Y[:, j, :], par("final", j), rstd[:], ALU.mult, ALU.mult).then_inc(out_made, 1)

        @block.gpsimd
        def _(pool):
            tt = nc.gpsimd.tensor_tensor
            links = Count(p_link)

            def link(ins):
                pool.wait_ge(p_link, links.inc(ins))

            for i in range(PAIRS):
                cos, sin, re, im = cos_t[i % 2], sin_t[i % 2], v_re[i % 2], v_im[i % 2]
                pool.wait_ge(scanned, i + 1)
                if i >= 1:
                    pool.wait_ge(states_read, i)
                tt(st_re[:], re, cos, ALU.mult)
                link(tt(st_t[:], im, sin, ALU.mult))
                link(tt(st_re[:], st_re[:], st_t[:], ALU.subtract))
                tt(st_im[:], re, sin, ALU.mult)
                link(tt(st_t[:], im, cos, ALU.mult))
                tt(st_im[:], st_im[:], st_t[:], ALU.add).then_inc(states_made, 1)
                pool.wait_ge(states_made, i + 1)

            pool.wait_ge(glu_done, 4)
            for g in range(POOL_TILES):
                pool.wait_ge(evacuated, N_POOL + g + 1)
                z = Y[:, 4 + g, :]
                src = z
                for k in range(g + 1):
                    sh, dst = 2 ** k, window[k % 2]
                    tt(dst[:, sh:], src[:, sh:], src[:, 0:SEQ - sh], ALU.add)
                    link(nc.gpsimd.tensor_copy(dst[:, 0:sh], src[:, 0:sh]))
                    src = dst
                link(nc.gpsimd.tensor_scalar(src, src, 0.5 ** (g + 1), None, ALU.mult))
                link(tt(src[:, 0:16], src[:, 0:16], consts[:, CC["corr"] + 16 * g:CC["corr"] + 16 * g + 16], ALU.mult))
                tt(z, src, z, ALU.subtract).then_inc(pooled, 1)
                pool.wait_ge(pooled, g + 1)


INPUTS = ["x", "p", "params", "consts", "iota", "causal", "s5_b", "s5_c", "w_in", "w_in_g", "w_a2", "w_glu",
          "w_pool", "w_out", "w_up", "w_down", "w_ple", "w_pg"]


def lay_out(x, p, norm_mix_w, w_in, s5_a_re, s5_a_im, s5_log_dt, s5_b_re, s5_b_im, s5_c_re, s5_c_im, s5_d,
            s5_w_glu, s5_b_glu, pool_w, pool_scale, gla_w_a2, gla_b_a, gla_norm_w, w_out, norm_ffn_w, w_up,
            conv_w, conv_b, w_down, norm_ple_w, w_ple, w_pg, final_norm_w):
    import numpy as np

    def tiles(w, m=P):
        k, n = w.shape
        return w.reshape(k // P, P, n // m, m).transpose(2, 1, 0, 3).reshape(n // m, P, k // P * m)

    def cols(v):
        return v.reshape(-1, P).T

    def features(a):
        return a.T.reshape(-1, P, a.shape[0]).transpose(1, 0, 2)

    out = {"x": features(x[0]), "p": features(p[0, 0])}
    wi = w_in[0]
    order = [(0, 512), (1024, 1536), (1536, 2048), (2048, 3072), (512, 1024), (3088, 4112)]
    out["w_in"] = tiles(np.concatenate([wi[:, a:b] for a, b in order], axis=1))
    out["w_in_g"] = tiles(wi[:, 3072:3088], RANK)[0]
    out["w_out"] = tiles(w_out[0])
    up = w_up[0]
    out["w_up"] = np.stack([tiles(up[:, :D_FF]), tiles(up[:, D_FF:])], axis=1).reshape(2 * FT, P, D)
    out["w_down"] = np.concatenate([tiles(w_down[0][q * QT * P:(q + 1) * QT * P]) for q in range(QUARTERS)])
    out["w_pg"] = tiles(w_pg[0])
    out["w_ple"] = tiles(w_ple[0]).reshape(2, PLE_PER, P, PLE_KT * P).transpose(0, 2, 1, 3).reshape(2, P, D)
    out["w_glu"] = s5_w_glu[0].reshape(S5_TILES, P, SEQ).transpose(1, 0, 2)
    out["w_pool"] = pool_w[0].transpose(1, 0, 2).reshape(P, POOL_TILES * P)
    out["w_a2"] = gla_w_a2[0]

    def states(a):
        return a.reshape(PAIRS, 2 * STATES).T

    dt = np.repeat(s5_log_dt[0][:, None], STATES, axis=1)
    out["params"] = np.concatenate(
        [cols(norm_mix_w[0]), cols(norm_ffn_w[0]), cols(norm_ple_w[0]), cols(final_norm_w), cols(s5_d[0]),
         cols(s5_b_glu[0]), cols(pool_scale[0]), cols(gla_b_a[0]), cols(gla_norm_w[0]), cols(conv_b[0]),
         conv_w[0].reshape(3, FT, P).transpose(2, 1, 0).reshape(P, 3 * FT), states(s5_a_re[0]),
         states(s5_a_im[0]), states(dt)], axis=1)

    def blocks(a):
        b = np.zeros((2, STATES, PAIRS, 2, 16), a.dtype)
        for g in range(2):
            b[g, :, :, g, :] = a[g::2].transpose(1, 0, 2)
        return b.reshape(P, 1, PAIRS, 32)

    out["s5_b"] = np.concatenate([blocks(s5_b_re[0]), blocks(s5_b_im[0])], axis=1).reshape(P, 2, SEQ)
    out["s5_c"] = np.concatenate([blocks(s5_c_re[0].transpose(0, 2, 1)), blocks(s5_c_im[0].transpose(0, 2, 1))],
                                 axis=1)
    corr = [[2.0 ** (g + 1) / min(t + 1, 2 ** (g + 1)) for t in range(16)] for g in range(POOL_TILES)]
    corr = np.broadcast_to(np.array(corr, np.float32).reshape(1, 64), (P, 64))
    out["consts"] = np.concatenate([np.eye(P, dtype=np.float32), corr], axis=1)
    out["iota"] = np.broadcast_to(np.arange(SEQ, dtype=np.float32), (P, SEQ))
    s, t = np.arange(P)[:, None], np.arange(P)[None, :]
    out["causal"] = ((s <= t) & (s // CHUNK == t // CHUNK)).astype(np.uint32)
    return {k: np.ascontiguousarray(v) for k, v in out.items()}


def kernel(**inputs):
    import numpy as np
    from concourse import bacc
    from concourse.bass_utils import run_bass_kernel_spmd

    arrays = lay_out(**{k: np.asarray(v) for k, v in inputs.items()})
    nc = bacc.Bacc("TRN2", target_bir_lowering=False, num_devices=1)
    A = {n: nc.dram_tensor(f"in_{n}", arrays[n].shape, mybir.dt.from_np(arrays[n].dtype), kind="ExternalInput").ap()
         for n in INPUTS}
    A["out"] = nc.dram_tensor("out_h", (P, KT, SEQ), F32, kind="ExternalOutput").ap()
    build(nc, A)
    r = run_bass_kernel_spmd(nc, [{f"in_{n}": arrays[n] for n in INPUTS}], core_ids=[0])
    out = r.results[0]["out_h"]
    return np.asarray(out).transpose(2, 1, 0).reshape(1, SEQ, D)
```

```python
from contextlib import ExitStack, contextmanager
import math

import concourse.bass as bass
from concourse import mybir

P = 128
SEQ = 512
D = 2048
KT = D // P
D_FF = 5632
FT = D_FF // P
QUARTERS = 4
QT = FT // QUARTERS
PLE_KT = 2
EPS = 1e-6
X_GROUPS = [0, 2, 6, 11, 16]
POOL_OUT = 5

S5_TILES = 4
PAIRS = 16
STATES = 64
POOL_TILES = 4
HEADS = 4
CHUNK = 64
CHUNKS = SEQ // CHUNK
DV = 256
RANK = 16

N_U, N_Q, N_K, N_G, N_V, N_POOL, N_R = 0, 4, 8, 12, 13, 21, 25
IN_TILES = 33
OUT0 = IN_TILES
FFN0 = OUT0 + KT
UP = 2 * QT
PER_QUARTER = UP + KT
PLE0 = FFN0 + QUARTERS * PER_QUARTER
PG0 = PLE0 + 2
PLE_PER = KT // 2

BU_SLOT = 4
U_SLOTS = (3, 6, 10, 14)
READ_SLOT = 6
HEAD_SLOT = 22

PC = {}
_at = 0
for _name, _n in (("mix", KT), ("ffn", KT), ("ple", KT), ("final", KT), ("d", 4), ("b_glu", 4), ("pscale", 4),
                  ("b_a", 4), ("gla_w", 2), ("conv_b", FT), ("conv_w", 3 * FT), ("a_re", PAIRS),
                  ("a_im", PAIRS), ("log_dt", PAIRS)):
    PC[_name] = _at
    _at += _n
N_PARAMS = _at
TWO_PI = 2.0 * math.pi
INV_2PI = 1.0 / TWO_PI
PI2_A = 6.28125
PI2_B = round((TWO_PI - PI2_A) * 2 ** 20) / 2 ** 20
PI2_C = TWO_PI - PI2_A - PI2_B
TO_INT = 1.5 * 2.0 ** 23
TO_2_16 = 1.5 * 2.0 ** 7
SIN_SCALE = 6.283185

F32 = mybir.dt.float32
F32R = mybir.dt.float32r
U32 = mybir.dt.uint32
ALU = mybir.AluOpType
ACT = mybir.ActivationFunctionType


class Count:

    def __init__(self, sem):
        self.sem, self.at, self.n = sem, 0, 0

    def inc(self, ins):
        ins.then_inc(self.sem, 1)
        self.at = self.at + 1
        self.n += 1
        return self.at


@contextmanager
def repeat(eng, times, **per):
    start = {k: c.at for k, (c, _) in per.items()}
    seen = {k: c.n for k, (c, _) in per.items()}
    with eng.Fori(0, times) as i:
        for k, (c, m) in per.items():
            c.at = start[k] + i * m
        yield i
    for k, (c, m) in per.items():
        assert c.n - seen[k] == m, (k, c.n - seen[k], m)
        c.at, c.n = start[k] + times * m, seen[k] + times * m


def build(nc, A):
    with ExitStack() as ctx:
        def sb(name, shape, dt=F32, where=ctx):
            return where.enter_context(nc.sbuf_tensor(name, shape, dt))

        def sem(name):
            return ctx.enter_context(nc.semaphore(name))

        xs_hi = sb("xs_hi", [P, KT, SEQ], F32R)
        xs_lo = sb("xs_lo", [P, KT, SEQ], F32R)
        w_raw = [sb(f"w_raw{s}", [P, D]) for s in range(2)]
        w_hi = [sb(f"w_hi{s}", [P, D], F32R) for s in range(2)]
        w_lo = [sb(f"w_lo{s}", [P, D], F32R) for s in range(2)]
        y_parts = ExitStack()
        U = sb("U", [P, KT, SEQ], F32R, y_parts)
        y_parts.close()
        Y = sb("Y", [P, KT, SEQ])
        rstd = sb("rstd", [P, SEQ])
        ones = sb("ones", [P, P])
        ident = sb("ident", [P, P])
        norm4 = sb("norm4", [P, 3, 4])
        params = sb("params_sb", [P, N_PARAMS])

        def par(name, i=0, n=1):
            if isinstance(i, int):
                return params[:, PC[name] + i:PC[name] + i + n]
            return params[:, bass.ds(i + PC[name], n)]

        mix = ExitStack()
        QKV = sb("QKV", [P, KT, SEQ], where=mix)
        corr = sb("corr_sb", [P, POOL_TILES, 16], where=mix)
        causal = sb("causal_sb", [P, P], U32, mix)
        w_a2 = sb("w_a2_sb", [2 * RANK, SEQ], where=mix)
        g_lr = sb("g_lr", [2 * RANK, SEQ], where=mix)
        s5 = ExitStack()
        BT_hi = [sb(f"BT_hi{c}", [P, S5_TILES, P], F32R, s5) for c in range(2)]
        BT_lo = [sb(f"BT_lo{c}", [P, S5_TILES, P], F32R, s5) for c in range(2)]
        CM = sb("CM", [P, 2, PAIRS, 32], where=s5)
        s5s = sb("s5s", [P, 17, PAIRS], where=s5)
        prod = sb("prod", [P, SEQ], where=s5)
        st_re = sb("st_re", [P, SEQ], where=s5)
        st_im = sb("st_im", [P, SEQ], where=s5)
        st_t = sb("st_t", [P, SEQ], where=s5)
        s5.close()
        gla = ExitStack()
        log_a = sb("log_a", [P, SEQ], where=gla)
        e_buf = sb("e_buf", [P, SEQ], where=gla)
        k_dec = sb("k_dec", [P, SEQ], where=gla)
        k_tok = sb("k_tok", [P, 4, P], where=gla)
        v_tok = sb("v_tok", [P, 4, DV], where=gla)
        sc = sb("sc", [P, 4, P], where=gla)
        S = sb("S", [P, CHUNKS - 1, DV], where=gla)
        decay = sb("decay", [P, CHUNKS], where=gla)
        gla.close()
        mix.close()
        outp = ExitStack()
        x_res = sb("x_res", [P, KT, SEQ], where=outp)
        outp.close()
        pg = ExitStack()
        ple = sb("ple", [P, KT, SEQ], where=pg)
        pg.close()
        mid_hi = sb("mid_hi", [P, QT, SEQ], F32R)
        mid_lo = sb("mid_lo", [P, QT, SEQ], F32R)
        parts_p = ExitStack()
        p_lo = sb("p_lo", [P, PLE_KT, SEQ], F32R, parts_p)
        p_hi = sb("p_hi", [P, PLE_KT, SEQ], F32R, parts_p)
        parts_p.close()
        conv_acc = sb("conv_acc", [P, SEQ])
        silu_g = sb("silu_g", [P, SEQ])
        conv_in = sb("conv_in", [P, SEQ + 2])
        val = sb("val", [P, SEQ])
        sq = sb("sq", [P, SEQ])
        ss = sb("ss", [P, SEQ])

        p_raw = [conv_acc[:], silu_g[:]]
        cos_t = [Y[:, 8 + b, :] for b in range(2)]
        sin_t = [Y[:, 10 + b, :] for b in range(2)]
        v_re = [Y[:, 12 + b, :] for b in range(2)]
        v_im = [Y[:, 14 + b, :] for b in range(2)]
        B_in = [QKV[:, 8 + c, :] for c in range(2)]
        B_bar = [QKV[:, 10 + c, :] for c in range(2)]
        B_prod = QKV[:, 12, :]
        x_sq = [QKV[:, 13, :], QKV[:, 15, :]]
        iota_t = QKV[:, 14, :]
        turns = QKV[:, 15, :]
        x_ss = QKV[:, 7, :]
        glu_gate = [Y[:, 9, :], Y[:, 10, :], Y[:, 11, :], Y[:, 15, :]]
        window = [Y[:, 12, :], Y[:, 13, :]]
        w_pool = Y[:, 14, :]
        k_tail = k_tok[:].rearrange("p j t -> p (j t)")
        x_diag = QKV[:, 5, :]

        bank = [ctx.enter_context(nc.psum_tensor(f"bank{b}", [P, SEQ], F32)) for b in range(8)]

        params_in = sem("params_in")
        x_in = [sem(f"x_in{g}") for g in range(4)]
        s5_in = sem("s5_in")
        wpool_in = sem("wpool_in")
        a2_in = sem("a2_in")
        glu_in = sem("glu_in")
        xres_in = [sem(f"xres_in{g}") for g in range(2)]
        p_in = sem("p_in")
        w_in = [sem(f"w_landed{s}") for s in range(2)]
        hi_begun = sem("hi_begun")
        lo_begun = sem("lo_begun")
        hi_made = sem("hi_made")
        lo_made = sem("lo_made")
        tile_done = sem("tile_done")
        evacuated = sem("evacuated")
        front_read = sem("front_read")
        xs_hi_made = sem("xs_hi_made")
        xs_lo_made = sem("xs_lo_made")
        ones_set = sem("ones_set")
        squared = sem("squared")
        sq_used = sem("sq_used")
        sum_spread = sem("sum_spread")
        var_made = sem("var_made")
        root_made = sem("root_made")
        diag_made = sem("diag_made")
        rstd_spread = sem("rstd_spread")
        rstd_made = sem("rstd_made")
        dt_made = sem("dt_made")
        exp_in = sem("exp_in")
        size_made = sem("size_made")
        step_turns = sem("step_turns")
        step_trig = sem("step_trig")
        inverse_made = sem("inverse_made")
        step_split = sem("step_split")
        bbar_made = sem("bbar_made")
        b_turned = sem("b_turned")
        bt_made = sem("bt_made")
        bt_hi_made = sem("bt_hi_made")
        u_hi_made = sem("u_hi_made")
        u_lo_made = sem("u_lo_made")
        cm_made = sem("cm_made")
        turns_made = sem("turns_made")
        trig_made = sem("trig_made")
        bu_made = sem("bu_made")
        rotated_in = sem("rotated_in")
        scanned = sem("scanned")
        states_made = sem("states_made")
        states_read = sem("states_read")
        y_added = sem("y_added")
        gelu_made = sem("gelu_made")
        glu_done = sem("glu_done")
        glu_sig = sem("glu_sig")
        y_s5_made = sem("y_s5_made")
        pooled = sem("pooled")
        pool_mixed = sem("pool_mixed")
        y_pool_made = sem("y_pool_made")
        logits_made = sem("logits_made")
        logits_out = sem("logits_out")
        soft_made = sem("soft_made")
        b_made = sem("b_made")
        decay_made = sem("decay_made")
        eb_made = sem("eb_made")
        ebn_made = sem("ebn_made")
        kd_made = sem("kd_made")
        diff_made = sem("diff_made")
        ebr_made = sem("ebr_made")
        kr_made = sem("kr_made")
        v_turned = sem("v_turned")
        v_tok_made = sem("v_tok_made")
        k_turned = sem("k_turned")
        k_tok_made = sem("k_tok_made")
        scores_made = sem("scores_made")
        sc_masked = sem("sc_masked")
        kv_made = sem("kv_made")
        S_made = sem("S_made")
        o_made = sem("o_made")
        o_out = sem("o_out")
        o_squared = sem("o_squared")
        o_summed = sem("o_summed")
        o_var = sem("o_var")
        o_root = sem("o_root")
        o_diag = sem("o_diag")
        o_spread = sem("o_spread")
        o_norm = sem("o_norm")
        r_silu = sem("r_silu")
        y_gla_made = sem("y_gla_made")
        sc_zeroed = sem("sc_zeroed")
        conv_made = sem("conv_made")
        silu_made = sem("silu_made")
        mid_made = sem("mid_made")
        mid_hi_made = sem("mid_hi_made")
        mid_lo_made = sem("mid_lo_made")
        p_hi_made = sem("p_hi_made")
        p_lo_made = sem("p_lo_made")
        ple_done = sem("ple_done")
        ple_out = sem("ple_out")
        gate_made = sem("gate_made")
        h_made = sem("h_made")
        scaled = sem("scaled")
        out_made = sem("out_made")
        out_pool_made = sem("out_pool_made")
        written = sem("written")
        v_link = sem("vector_link")
        a_link = sem("scalar_link")
        p_link = sem("gpsimd_link")

        W_FULL, W_G, W_DOWN = D, KT * RANK, QT * P
        HALF_Q = PER_QUARTER // 2

        def landed(eng, c, e=0):
            eng.wait_ge(w_in[c % 2], (e + c // 2 + 1) * 16)

        def in_width(n):
            return W_G if n == N_G else W_FULL

        def in_bank(n):
            return n if n < 4 else n % 2

        def kv_place(c):
            return bank[(3, 4, 6, 2)[2 * (c % 2) + c // 4]][:, (c // 2 % 2) * DV:(c // 2 % 2 + 1) * DV]

        block = ctx.enter_context(nc.Block())

        @block.sync
        def _(sp):
            def weights(c, e, src, width, free=True):
                if free:
                    sp.wait_ge(lo_made, 2 * e + c - 1)
                sp.dma_start(w_raw[c % 2][:, 0:width], src).then_inc(w_in[c % 2], 16)

            for n in range(IN_TILES):
                src = A["w_in_g"] if n == N_G else A["w_in"][n - (n > N_G)]
                if n == 0:
                    sp.dma_start(params[:], A["params"]).then_inc(params_in, 16)
                    for g in range(4):
                        gs = slice(X_GROUPS[g], X_GROUPS[g + 1])
                        sp.dma_start(Y[:, gs, :], A["x"][:, gs, :]).then_inc(x_in[g], 16)
                        if g == 0:
                            weights(n, 0, src, D, free=False)
                else:
                    weights(n, 0, src, in_width(n), free=n >= 2)
                if n == 1:
                    sp.dma_start(ident[:], A["ident"]).then_inc(s5_in, 16)
                    sp.dma_start(iota_t, A["iota"]).then_inc(s5_in, 16)
                    for c in range(2):
                        sp.dma_start(B_in[c], A["s5_b"][:, c, :]).then_inc(s5_in, 16)
                    sp.dma_start(CM[:], A["s5_c"]).then_inc(s5_in, 16)
                    sp.dma_start(causal[:], A["causal"]).then_inc(a2_in, 16)
                    sp.dma_start(w_a2[:], A["w_a2"]).then_inc(a2_in, 16)
                    sp.dma_start(corr[:], A["corr"]).then_inc(a2_in, 16)
                if n == HEAD_SLOT + 2:
                    sp.wait_ge(states_made, PAIRS)
                    sp.dma_start(Y[:, 12:16, :], A["w_glu"]).then_inc(glu_in, 16)
                if n == HEAD_SLOT + 5:
                    sp.wait_ge(glu_done, 4)
                    sp.dma_start(w_pool, A["w_pool"]).then_inc(wpool_in, 16)
            for s in range(2):
                weights(OUT0 + s, 0, A["w_out"][s], W_FULL)
            sp.wait_ge(y_gla_made, 2 * HEADS)
            sp.dma_start(x_res[:, 0:2, :], A["x"][:, 0:2, :]).then_inc(xres_in[0], 16)

            def out_pair(j, r):
                i = 2 * j + r
                for s in range(2):
                    weights(OUT0 + s, i, A["w_out"][2 * i + s], W_FULL)
                two = slice(2 * i, 2 * i + 2) if isinstance(i, int) else bass.ds(2 * i, 2)
                sp.dma_start(x_res[:, two, :], A["x"][:, two, :]).then_inc(xres_in[r % 2], 16)

            with sp.Fori(0, KT // 4 - 1) as j:
                out_pair(j, 1)
                out_pair(j, 2)
            out_pair(KT // 4 - 1, 1)
            with sp.Fori(0, QUARTERS) as q:
                with sp.Fori(0, QT) as i:
                    for s in range(2):
                        weights(FFN0 + s, q * HALF_Q + i, A["w_up"][q * UP + 2 * i + s], W_FULL)
                with sp.Fori(0, KT // 2) as i:
                    for s in range(2):
                        weights(FFN0 + UP + s, q * HALF_Q + i, A["w_down"][q * KT + 2 * i + s], W_DOWN)
            sp.wait_ge(mid_lo_made, FT)
            for k in range(PLE_KT):
                sp.dma_start(p_raw[k], A["p"][:, k, :]).then_inc(p_in, 16)
            for s in range(2):
                weights(PLE0 + s, 0, A["w_ple"][s], W_FULL)
            with sp.Fori(0, KT // 2) as i:
                for s in range(2):
                    weights(PG0 + s, i, A["w_pg"][2 * i + s], W_FULL)
            for t in range(KT):
                from_pool = t % 3 == 2 and t // 3 < POOL_OUT
                j = t // 3 if from_pool else POOL_OUT + t - min((t + 1) // 3, POOL_OUT)
                sp.wait_ge(*((out_pool_made, j + 1) if from_pool else (out_made, j + 1 - POOL_OUT)))
                sp.dma_start(A["out"][:, j, :], Y[:, j, :]).then_inc(written, 16)
            sp.wait_ge(written, 16 * KT)

        @block.tensor
        def _(pe):
            def product(out, w_h, w_l, x_h, x_l, first, last):
                nc.tensor.matmul(out, w_h, x_h, start=first, stop=False)
                nc.tensor.matmul(out, w_h, x_l, start=False, stop=False)
                return nc.tensor.matmul(out, w_l, x_h, start=False, stop=last)

            def rank_tile(slot, out):
                for k in range(KT):
                    w = w_hi[slot][:, 2 * k * RANK:2 * (k + 1) * RANK]
                    nc.tensor.matmul(out, w, xs_hi[:, k, :], start=k == 0, stop=False)
                    last = nc.tensor.matmul(out, w, xs_lo[:, k, :], start=False, stop=k == KT - 1)
                last.then_inc(tile_done, 1)

            def tile(slot, out, x_h, x_l, kts, before=None, front=False):
                for k in range(kts):
                    if before is not None:
                        before(k)
                    ks = slice(k * P, (k + 1) * P)
                    last = product(out, w_hi[slot][:, ks], w_lo[slot][:, ks], x_h[:, k, :], x_l[:, k, :],
                                   k == 0, k == kts - 1)
                    if front and k == kts // 2 - 1:
                        last.then_inc(front_read, 1)
                last.then_inc(tile_done, 1)

            def spread_sum(n_squares, src, out):
                pe.wait_ge(sq_used, n_squares)
                nc.tensor.matmul(out[:], ones[:], src, start=True, stop=True).then_inc(sum_spread, 1)

            def sum_tokens(n_squares, parts, out, done):
                if n_squares:
                    pe.wait_ge(sq_used, n_squares)
                for j in range(4):
                    for e, src in enumerate(parts):
                        m = nc.tensor.matmul(out[:, j:j + 1], src[:, j * P:(j + 1) * P], ones[:, 0:1],
                                             start=e == 0, stop=e == len(parts) - 1)
                m.then_inc(done, 1)

            def spread(made, n, src, out, done):
                pe.wait_ge(made, n)
                nc.tensor.matmul(out[:], ones[:], src, start=True, stop=True).then_inc(done, 1)

            def turn_b():
                pe.wait_ge(bbar_made, 1)
                for c in range(2):
                    for j in range(S5_TILES):
                        js = slice(j * P, (j + 1) * P)
                        t = nc.tensor.transpose(bank[4 + c][:, js], B_bar[c][:, js], ident[:])
                t.then_inc(b_turned, 1)

            def bu(i):
                c, rows = i // 4, slice(32 * (i % 4), 32 * (i % 4) + 32)
                pe.wait_ge(bt_made, 2)
                pe.wait_ge(u_lo_made, c + 1)
                pe.wait_ge(evacuated, 4)
                if i >= 2:
                    pe.wait_ge(rotated_in, i - 1)
                for b in range(2):
                    m = product(bank[2 + 2 * (i % 2) + b][:], BT_hi[b][rows, c, :], BT_lo[b][rows, c, :],
                                U[rows, 4 + c % 2, :], U[rows, 6 + c % 2, :], True, True)
                m.then_inc(bu_made, 1)

            def read_states(i):
                c, j = i // 4, i % 4
                pe.wait_ge(cm_made, 1)
                pe.wait_ge(states_made, i + 1)
                if c >= 2:
                    pe.wait_ge(y_added, c - 1)
                if i == 4:
                    pe.wait_ge(rstd_made, 1)
                out = bank[6 + c % 2][32 * j:32 * j + 32, :]
                nc.tensor.matmul(out, CM[:, 0, i, :], st_re[:], start=True, stop=False, skip_group_check=True)
                nc.tensor.matmul(out, CM[:, 1, i, :], st_im[:], start=False, stop=True,
                                 skip_group_check=True).then_inc(states_read, 1)

            def glu(j):
                if j == 0:
                    pe.wait_ge(gelu_made, S5_TILES)
                    pe.wait_ge(glu_in, 16)
                if j == 1:
                    pe.wait_ge(logits_out, 1)
                if j == 2:
                    pe.wait_ge(sc_masked, 1)
                if j == 3:
                    pe.wait_ge(glu_sig, 3)
                for k in range(S5_TILES):
                    m = nc.tensor.matmul(bank[(6, 7, 5, 5)[j]][:], Y[:, 12 + k, j * P:(j + 1) * P], Y[:, k, :],
                                         start=k == 0, stop=k == S5_TILES - 1)
                m.then_inc(glu_done, 1)

            def mix_pool(g):
                pe.wait_ge(pooled, g + 1)
                if g == 0:
                    pe.wait_ge(wpool_in, 16)
                if g % 2:
                    pe.wait_ge(y_pool_made, g)
                else:
                    pe.wait_ge(sc_masked, g // 2 + 2)
                nc.tensor.matmul(bank[5][:], w_pool[:, g * P:(g + 1) * P], Y[:, 4 + g, :], start=True,
                                 stop=True).then_inc(pool_mixed, 1)

            def head_logits(h):
                if h == 0:
                    pe.wait_ge(a2_in, 48)
                    pe.wait_ge(y_added, 4)
                if h == 1:
                    pe.wait_ge(glu_sig, 2)
                if h >= 2:
                    pe.wait_ge(o_out, h - 1)
                nc.tensor.matmul(bank[7][:], w_a2[:, h * P:(h + 1) * P], g_lr[:], start=True,
                                 stop=True).then_inc(logits_made, 1)

            def head_turn(h):
                if h == 0:
                    pe.wait_ge(rotated_in, PAIRS)
                    pe.wait_ge(evacuated, N_V + 8)
                else:
                    pe.wait_ge(S_made, h)
                for e in range(2):
                    for j in range(4):
                        js = slice(j * P, (j + 1) * P)
                        m = nc.tensor.transpose(bank[3 + e][:, js], QKV[:, 8 + 2 * h + e, js], ident[:])
                m.then_inc(v_turned, 1)
                pe.wait_ge(kr_made, h + 1)
                if h >= 2:
                    pe.wait_ge(o_norm, h - 1)
                for j in range(4):
                    js = slice(j * P, (j + 1) * P)
                    m = nc.tensor.transpose(bank[2][:, js], QKV[:, 4 + h, js], ident[:])
                m.then_inc(k_turned, 1)
                if h == 1:
                    pe.wait_ge(glu_sig, 4)
                if h >= 2:
                    pe.wait_ge(y_pool_made, 2 * h - 2)
                for j in range(4):
                    ts = slice(j * P, (j + 1) * P)
                    m = nc.tensor.matmul(bank[5][:, ts], k_dec[:, ts], QKV[:, h, ts], start=True, stop=True)
                m.then_inc(scores_made, 1)

            def head_kv(h):
                pe.wait_ge(k_tok_made, h + 1)
                pe.wait_ge(v_tok_made, h + 1)
                if h == 0:
                    pe.wait_ge(glu_sig, 1)
                else:
                    pe.wait_ge(o_out, h)
                for c in range(CHUNKS - 1):
                    rows = slice(CHUNK * (c % 2), CHUNK * (c % 2) + CHUNK)
                    m = nc.tensor.matmul(kv_place(c), k_tok[rows, c // 2, :], v_tok[rows, c // 2, :], start=True, stop=True)
                m.then_inc(kv_made, 1)

            def head_o(h):
                pe.wait_ge(sc_masked, h + 1)
                pe.wait_ge(S_made, h + 1)
                pe.wait_ge(logits_out, min(h + 2, HEADS))
                for e in range(2):
                    es = slice(e * P, (e + 1) * P)
                    for j in range(4):
                        nc.tensor.matmul(bank[6 + e][:, j * P:(j + 1) * P], v_tok[:, j, es], sc[:, j, :],
                                         start=True, stop=False, skip_group_check=True)
                        for c in (2 * j, 2 * j + 1):
                            if c >= 1:
                                ts = slice(c * CHUNK, (c + 1) * CHUNK)
                                m = nc.tensor.matmul(bank[6 + e][:, ts], S[:, c - 1, es], QKV[:, h, ts],
                                                     start=False, stop=c % 2 == 1, skip_group_check=True)
                m.then_inc(o_made, 1)

            def head_norm(h):
                pe.wait_ge(o_squared, h + 1)
                pe.wait_ge(S_made, min(h + 2, HEADS))
                if h >= 1:
                    pe.wait_ge(o_norm, h)
                sum_tokens(0, [QKV[:, h, :], QKV[:, 4 + h, :]], bank[2], o_summed)

            norm_slot = [HEAD_SLOT + 5, HEAD_SLOT + 7, HEAD_SLOT + 9, HEAD_SLOT + 10]

            for n in range(IN_TILES):
                pe.wait_ge(*((lo_begun, n + 1) if n < 2 else (lo_made, n + 1)))
                if n >= 4:
                    pe.wait_ge(evacuated, n - 1)

                def before(k, n=n):
                    if n < 2 and k == KT // 2:
                        pe.wait_ge(lo_made, n + 1)
                    if n == 0:
                        pe.wait_ge(xs_lo_made, k + 1)
                    if n == 2 and k == 8:
                        pe.wait_ge(ones_set, 1)
                        sum_tokens(KT, [x_ss], bank[7], sum_spread)
                    if n == 3 and k == 1:
                        spread(diag_made, 1, x_diag, bank[7], rstd_spread)
                    if k == KT // 2:
                        if n == HEAD_SLOT + 3:
                            glu(3)
                        if n in (HEAD_SLOT + 5, HEAD_SLOT + 7):
                            mix_pool(n - HEAD_SLOT - 4)
                        if n in norm_slot:
                            head_norm(norm_slot.index(n))
                    if n in norm_slot and k == (KT - 4 if n == IN_TILES - 1 else KT - 1):
                        h = norm_slot.index(n)
                        spread(o_diag, h + 1, QKV[:, h, :], bank[2], o_spread)

                if n == N_G:
                    rank_tile(n % 2, bank[in_bank(n)][0:2 * RANK, :])
                else:
                    tile(n % 2, bank[in_bank(n)][:], xs_hi, xs_lo, KT, before, front=n == IN_TILES - 1)
                if n == 3:
                    turn_b()
                if READ_SLOT <= n < READ_SLOT + PAIRS:
                    read_states(n - READ_SLOT)
                if BU_SLOT <= n < BU_SLOT + PAIRS:
                    bu(n - BU_SLOT)
                s = n - HEAD_SLOT
                if s >= 3 and s % 2 == 1:
                    head_o((s - 3) // 2)
                if s in (0, 2, 4, 6):
                    head_logits(s // 2)
                if s == 1:
                    glu(0)
                    glu(1)
                if s in (1, 3, 5, 7):
                    head_turn((s - 1) // 2)
                if s in (2, 4, 6, 8):
                    head_kv((s - 2) // 2)
                if s == 2:
                    glu(2)
                if s in (4, 6):
                    mix_pool(s - 4)

            for n in (OUT0, OUT0 + 1):
                pe.wait_ge(lo_made, n + 1)
                pe.wait_ge(evacuated, n - 1)

                def before(k, n=n):
                    if n == OUT0:
                        pe.wait_ge(xs_lo_made, KT + k + 1)

                tile(n % 2, bank[n % 2][:], xs_hi, xs_lo, KT, before)
            with pe.Fori(1, KT // 2) as i:
                for s in range(2):
                    pe.wait_ge(lo_made, 2 * i + (OUT0 + s + 1))
                    pe.wait_ge(evacuated, 2 * i + (OUT0 + s - 1))
                    tile((OUT0 + s) % 2, bank[(OUT0 + s) % 2][:], xs_hi, xs_lo, KT, front=s == 1)

            def up_pair(q, i):
                first = isinstance(i, int)
                for s in range(2):
                    n = PER_QUARTER * q + 2 * i + (FFN0 + s)
                    pe.wait_ge(lo_made, n + 1)
                    pe.wait_ge(evacuated, n - 1)

                    def before(k, s=s):
                        if s == 0:
                            pe.wait_ge(xs_lo_made, 2 * KT + k + 1)
                        if first and s == 0 and k == 8:
                            sum_tokens(2 * KT, [ss], bank[2], sum_spread)
                        if first and s == 1 and k == 6:
                            spread(diag_made, 2, val[:], bank[2], rstd_spread)

                    tile((FFN0 + s) % 2, bank[(FFN0 + s) % 2][:], xs_hi, xs_lo, KT, before)

            def down_tiles(q):
                with pe.Fori(0, KT // 2) as i:
                    for s in range(2):
                        n = PER_QUARTER * q + 2 * i + (FFN0 + UP + s)
                        pe.wait_ge(lo_made, n + 1)
                        pe.wait_ge(evacuated, n - 1)

                        def before(k, s=s):
                            if s == 0 and k in (0, QT - 1):
                                pe.wait_ge(mid_lo_made, QT * q + (QT - 1 if k == 0 else QT))

                        tile((FFN0 + UP + s) % 2, bank[(FFN0 + UP + s) % 2][:], mid_hi, mid_lo, QT, before)

            up_pair(0, 0)
            with pe.Fori(1, QT) as i:
                up_pair(0, i)
            down_tiles(0)
            with pe.Fori(1, QUARTERS) as q:
                with pe.Fori(0, QT) as i:
                    up_pair(q, i)
                down_tiles(q)

            pe.wait_ge(p_lo_made, PLE_KT)
            for s in range(2):
                pe.wait_ge(lo_made, PLE0 + s + 1)
                slot = (PLE0 + s) % 2
                for u in range(PLE_PER):
                    j = PLE_PER * s + u
                    if j >= 4:
                        pe.wait_ge(ple_out, j - 3)
                    for k in range(PLE_KT):
                        ks = slice((u * PLE_KT + k) * P, (u * PLE_KT + k + 1) * P)
                        m = product(bank[3 + j % 4][:], w_hi[slot][:, ks], w_lo[slot][:, ks], p_hi[:, k, :],
                                    p_lo[:, k, :], k == 0, k == PLE_KT - 1)
                    m.then_inc(ple_done, 1)
            spread_sum((2 + QUARTERS) * KT, ss[:], bank[2])
            with pe.Fori(0, KT // 2) as i:
                for s in range(2):
                    pe.wait_ge(lo_made, 2 * i + (PG0 + s + 1))
                    pe.wait_ge(evacuated, 2 * i + (PG0 - 2 + s - 1))
                    before = (lambda k: pe.wait_ge(xs_lo_made, 3 * KT + k + 1)) if s == 0 else None
                    tile((PG0 + s) % 2, bank[(PG0 + s) % 2][:], xs_hi, xs_lo, KT, before)
            pe.wait_ge(squared, (3 + QUARTERS) * KT)
            sum_tokens((3 + QUARTERS) * KT - 1, [ss, sq], bank[2], sum_spread)
            spread(diag_made, 3, val[:], bank[2], rstd_spread)

        @block.scalar
        def _(act):
            link_count = Count(a_link)

            def link(ins):
                act.wait_ge(a_link, link_count.inc(ins))

            def w_half(c, e=0, width=W_FULL, used=0):
                landed(act, c, e)
                act.wait_ge(tile_done, 2 * e + (c - 1 - used))
                nc.scalar.activation(w_hi[c % 2][:, 0:width], w_raw[c % 2][:, 0:width], ACT.Copy).then_inc(hi_made, 1)

            def w_half_halves(n):
                landed(act, n)
                for half in range(2):
                    hs = slice(half * D // 2, (half + 1) * D // 2)
                    nc.scalar.activation(w_hi[n][:, hs], w_raw[n][:, hs],
                                         ACT.Copy).then_inc((hi_begun, hi_made)[half], 1)

            def w_half_rank():
                landed(act, N_G)
                act.wait_ge(tile_done, N_G - 1)
                w = w_hi[N_G % 2][:, 0:2 * W_G].rearrange("p (k e m) -> p k e m", e=2, m=RANK)
                raw = w_raw[N_G % 2][:, 0:W_G].rearrange("p (k m) -> p k m", m=RANK)
                nc.scalar.activation(w[:, :, 0, :], raw, ACT.Copy).then_inc(hi_made, 1)

            def w_first(c):
                landed(act, c)
                nc.scalar.activation(w_hi[c % 2][:], w_raw[c % 2][:], ACT.Copy).then_inc(hi_made, 1)

            def x_half(k, gain=None):
                scale = 1.0 if gain is None else par(gain, k)
                nc.scalar.activation(xs_hi[:, k, :], Y[:, k, :], ACT.Identity, scale=scale).then_inc(xs_hi_made, 1)

            def square(src, used, made):
                act.wait_ge(evacuated, made)
                act.wait_ge(sq_used, used)
                nc.scalar.activation(sq[:], src, ACT.Square).then_inc(squared, 1)

            def root(n, dst, src):
                act.wait_ge(var_made, n + 1)
                nc.scalar.activation(dst, src, ACT.Sqrt).then_inc(root_made, 1)

            def u_half(c):
                act.wait_ge(evacuated, c + 1)
                if c >= 2:
                    act.wait_ge(bu_made, 4 * (c - 1))
                nc.scalar.activation(U[:, 4 + c % 2, :], Y[:, c, :], ACT.Copy).then_inc(u_hi_made, 1)

            def trig(i):
                act.wait_ge(turns_made, i + 1)
                if i < 2:
                    act.wait_ge(tile_done, 1)
                else:
                    act.wait_ge(states_made, i - 1)
                nc.scalar.activation(sin_t[i % 2], turns, ACT.Sin, scale=SIN_SCALE)
                link(nc.scalar.activation(cos_t[i % 2], turns, ACT.Sin, scale=math.pi))
                nc.scalar.activation(cos_t[i % 2], cos_t[i % 2], ACT.Square).then_inc(trig_made, 1)

            def head_soft(h):
                act.wait_ge(logits_made, h + 1)
                if h >= 1:
                    act.wait_ge(kr_made, h)
                nc.scalar.activation(e_buf[:], bank[7][:], ACT.Abs, bias=par("b_a", h))
                nc.scalar.activation(log_a[:], bank[7][:], ACT.Identity, bias=par("b_a", h)).then_inc(logits_out, 1)
                act.wait_ge(logits_out, h + 1)
                link(nc.scalar.activation(e_buf[:], e_buf[:], ACT.Exp, scale=-1.0))
                nc.scalar.activation(e_buf[:], e_buf[:], ACT.Ln, bias=1.0).then_inc(soft_made, 1)

            def head_decay(h):
                act.wait_ge(b_made, h + 1)
                nc.scalar.activation(e_buf[:], log_a[:], ACT.Exp, scale=1 / 16).then_inc(eb_made, 1)
                nc.scalar.activation(k_dec[:], log_a[:], ACT.Exp, scale=-1 / 16).then_inc(ebn_made, 1)
                act.wait_ge(diff_made, h + 1)
                nc.scalar.activation(k_tail, k_tail, ACT.Exp, scale=1 / 16).then_inc(ebr_made, 1)
                nc.scalar.activation(decay[:], log_a[:, CHUNK - 1:SEQ:CHUNK], ACT.Exp, scale=1 / 16).then_inc(decay_made, 1)

            def head_tokens(h):
                act.wait_ge(v_turned, h + 1)
                for e in range(2):
                    m = nc.scalar.activation(v_tok[:, :, e * P:(e + 1) * P],
                                             bank[3 + e][:].rearrange("p (j d) -> p j d", j=4), ACT.Copy)
                m.then_inc(v_tok_made, 1)
                act.wait_ge(k_turned, h + 1)
                nc.scalar.activation(k_tok[:], bank[2][:].rearrange("p (j d) -> p j d", j=4),
                                     ACT.Copy).then_inc(k_tok_made, 1)

            def head_out(h):
                act.wait_ge(o_made, h + 1)
                for e in range(2):
                    m = nc.scalar.activation(QKV[:, 8 + 2 * h + e, :], bank[6 + e][:], ACT.Copy)
                m.then_inc(o_out, 1)
                act.wait_ge(o_out, h + 1)
                for e in range(2):
                    m = nc.scalar.activation(QKV[:, h + 4 * e, :], QKV[:, 8 + 2 * h + e, :], ACT.Square)
                m.then_inc(o_squared, 1)

            def head_root(h):
                act.wait_ge(o_var, h + 1)
                nc.scalar.activation(norm4[:, 1, :], norm4[:, 0, :], ACT.Sqrt).then_inc(o_root, 1)

            def gate_glu(j):
                act.wait_ge(glu_done, j + 1)
                nc.scalar.activation(glu_gate[j], bank[(6, 7, 5, 5)[j]][:], ACT.Sigmoid,
                                     bias=par("b_glu", j)).then_inc(glu_sig, 1)

            def silu_r(k):
                act.wait_ge(evacuated, N_R + k + 1)
                nc.scalar.activation(Y[:, 8 + k, :], Y[:, 8 + k, :], ACT.Silu).then_inc(r_silu, 1)

            act.wait_ge(params_in, 16)
            nc.scalar.activation(s5s[:, 0, :], par("log_dt", 0, PAIRS), ACT.Exp).then_inc(dt_made, 1)
            for g in range(4):
                act.wait_ge(x_in[g], 16)
                for k in range(X_GROUPS[g], X_GROUPS[g + 1]):
                    x_half(k, "mix")
                if g == 0:
                    w_half_halves(0)
            w_half_halves(1)
            act.wait_ge(exp_in, 1)
            nc.scalar.activation(s5s[:, 3, :], s5s[:, 1, :], ACT.Exp).then_inc(size_made, 1)
            for k in range(KT):
                if k >= 2:
                    act.wait_ge(sq_used, k - 1)
                nc.scalar.activation(x_sq[k % 2], Y[:, k, :], ACT.Square).then_inc(squared, 1)
                if k == KT // 2 - 1:
                    w_half(2)
                    act.wait_ge(step_turns, 1)
                    nc.scalar.activation(s5s[:, 9, :], s5s[:, 6, :], ACT.Sin, scale=SIN_SCALE)
                    nc.scalar.activation(s5s[:, 10, :], s5s[:, 6, :], ACT.Sin, scale=math.pi).then_inc(step_trig, 1)
            w_half(3)
            root(0, norm4[:, 1, :], norm4[:, 0, :])
            act.wait_ge(rstd_spread, 1)
            nc.scalar.activation(rstd[:], bank[7][:], ACT.Copy).then_inc(rstd_made, 1)
            for n in range(2, IN_TILES):
                s = n - HEAD_SLOT
                if s == 3:
                    gate_glu(3)
                if s in (5, 7, 9, 10):
                    head_root(min((s - 5) // 2, 3) if s < 10 else 3)
                if s in (0, 2, 4, 6):
                    head_soft(s // 2)
                if n + 2 == N_G:
                    w_half_rank()
                elif n < IN_TILES - 1:
                    w_half(n + 2)
                if n == 3:
                    act.wait_ge(b_turned, 1)
                    for c in range(2):
                        nc.scalar.activation(BT_hi[c][:], bank[4 + c][:].rearrange("p (j d) -> p j d", j=4),
                                             ACT.Copy).then_inc(bt_hi_made, 1)
                if n in U_SLOTS:
                    u_half(U_SLOTS.index(n))
                if BU_SLOT - 1 <= n < BU_SLOT - 1 + PAIRS:
                    trig(n - BU_SLOT + 1)
                if s == 0:
                    for c in range(S5_TILES):
                        act.wait_ge(y_added, c + 1)
                        nc.scalar.activation(Y[:, c, :], Y[:, c, :], ACT.Gelu_apprx_tanh).then_inc(gelu_made, 1)
                if s >= 3 and s % 2 == 1:
                    head_out((s - 3) // 2)
                if s == 2:
                    gate_glu(2)
                if s in (0, 2, 4, 6):
                    head_decay(s // 2)
                if s in (1, 3, 5, 7):
                    head_tokens((s - 1) // 2)
                if s == 1:
                    gate_glu(0)
                    gate_glu(1)
                if s in (5, 7, 9):
                    silu_r(s - 5)
                    silu_r(s - 4)
            silu_r(6)
            act.wait_ge(front_read, 1)
            for k in range(KT):
                if k == KT // 2:
                    act.wait_ge(tile_done, IN_TILES)
                if k == KT - 2:
                    silu_r(7)
                    w_half(IN_TILES + 1)
                if k < 4:
                    act.wait_ge(y_s5_made, 4)
                elif k < 8:
                    act.wait_ge(y_pool_made, 4)
                else:
                    act.wait_ge(y_gla_made, k - 7)
                x_half(k)
            with act.Fori(0, KT // 2 - 1) as i:
                for s in range(2):
                    w_half(OUT0 + 2 + s, i)
                    square(Y[:, bass.ds(2 * i + s, 1), :], 2 * i + (KT + s), 2 * i + (OUT0 + s + 1))
            w_half(FFN0)
            square(Y[:, KT - 2, :], 2 * KT - 2, FFN0 - 1)
            act.wait_ge(front_read, KT // 2)
            for k in range(KT):
                if k == KT // 2:
                    act.wait_ge(tile_done, FFN0)
                x_half(k, "ffn")
                if k == KT // 2:
                    square(Y[:, KT - 1, :], 2 * KT - 1, FFN0)
                if k == KT - 4:
                    w_half(FFN0 + 1)
            root(1, norm4[:, 1, :], norm4[:, 0, :])
            act.wait_ge(rstd_spread, 2)
            nc.scalar.activation(rstd[:], bank[2][:], ACT.Copy).then_inc(rstd_made, 1)

            def up_pair(q, i, width):
                e = q * HALF_Q + i
                f = q * QT + i
                w_half(FFN0 + 2, e, width)
                act.wait_ge(conv_made, f + 1)
                nc.scalar.activation(silu_g[:], conv_acc[:], ACT.Silu).then_inc(silu_made, 1)
                act.wait_ge(mid_made, f + 1)
                dst = mid_hi[:, i, :] if isinstance(i, int) else mid_hi[:, bass.ds(i, 1), :]
                nc.scalar.activation(dst, val[:], ACT.Copy).then_inc(mid_hi_made, 1)
                w_half(FFN0 + 3, e, width)

            def quarter(q, last):
                with act.Fori(0, QT - 1) as i:
                    up_pair(q, i, W_FULL)
                up_pair(q, QT - 1, W_DOWN)
                with act.Fori(0, KT // 2 - 1) as i:
                    for s in range(2):
                        w_half(FFN0 + UP + 2 + s, q * HALF_Q + i, W_DOWN)
                        square(Y[:, bass.ds(2 * i + s, 1), :], KT * q + 2 * i + (2 * KT + s),
                               PER_QUARTER * q + 2 * i + (FFN0 + UP + s + 1))
                if last:
                    act.wait_ge(p_in, 16 * PLE_KT)
                    for k in range(PLE_KT):
                        nc.scalar.activation(p_hi[:, k, :], p_raw[k], ACT.Copy).then_inc(p_hi_made, 1)
                for s in range(2):
                    w_half(FFN0 + PER_QUARTER + s, q * HALF_Q)
                    square(Y[:, KT - 2 + s, :], KT * q + (3 * KT - 2 + s), PER_QUARTER * q + (FFN0 + PER_QUARTER - 1 + s))

            with act.Fori(0, QUARTERS - 1) as q:
                quarter(q, False)
            quarter(QUARTERS - 1, True)
            for k in range(KT):
                x_half(k, "ple")
                if k == 10:
                    landed(act, PG0)
                    act.wait_ge(ple_done, PLE_PER)
                    nc.scalar.activation(w_hi[PG0 % 2][:], w_raw[PG0 % 2][:], ACT.Copy).then_inc(hi_made, 1)
                act.wait_ge(ple_done, k + 1)
                nc.scalar.activation(ple[:, k, :], bank[3 + k % 4][:], ACT.Copy).then_inc(ple_out, 1)
            w_first(PG0 + 1)
            root(2, rstd[:], val[:])

            def gate(i, s, last):
                j = 2 * i + s
                if not last:
                    w_half(PG0 + 2 + s, i, used=2)
                act.wait_ge(evacuated, j + (PG0 - 2 + 1))
                nc.scalar.activation(conv_acc[:], conv_acc[:], ACT.Sigmoid).then_inc(gate_made, 1)
                act.wait_ge(h_made, j + 1)
                act.wait_ge(sq_used, j + (2 + QUARTERS) * KT)
                src = Y[:, j, :] if isinstance(i, int) else Y[:, bass.ds(j, 1), :]
                nc.scalar.activation(sq[:], src, ACT.Square).then_inc(squared, 1)

            with act.Fori(0, KT // 2 - 1) as i:
                for s in range(2):
                    gate(i, s, False)
            for j in range(POOL_OUT):
                nc.scalar.activation(Y[:, j, :], Y[:, j, :], ACT.Identity, scale=par("final", j)).then_inc(scaled, 1)
            for s in range(2):
                gate(KT // 2 - 1, s, True)
            root(3, norm4[:, 1, :], norm4[:, 0, :])
            act.wait_ge(rstd_spread, 3)
            nc.scalar.activation(rstd[:], bank[2][:], ACT.Copy).then_inc(rstd_made, 1)

        @block.vector
        def _(dve):
            tt, ts, stt = nc.vector.tensor_tensor, nc.vector.tensor_scalar, nc.vector.scalar_tensor_tensor
            links = Count(v_link)

            def link(ins):
                dve.wait_ge(v_link, links.inc(ins))

            def w_rest(c, e=0, width=W_FULL):
                dve.wait_ge(hi_made, 2 * e + (c + 1))
                tt(w_lo[c % 2][:, 0:width], w_raw[c % 2][:, 0:width], w_hi[c % 2][:, 0:width].bitcast(F32),
                   ALU.subtract).then_inc(lo_made, 1)

            def w_rest_halves(n):
                for half in range(2):
                    dve.wait_ge((hi_begun, hi_made)[half], n + 1)
                    hs = slice(half * D // 2, (half + 1) * D // 2)
                    tt(w_lo[n][:, hs], w_raw[n][:, hs], w_hi[n][:, hs].bitcast(F32),
                       ALU.subtract).then_inc((lo_begun, lo_made)[half], 1)

            def w_rest_rank():
                dve.wait_ge(hi_made, N_G + 1)
                w = w_hi[N_G % 2][:, 0:2 * W_G].rearrange("p (k e m) -> p k e m", e=2, m=RANK)
                raw = w_raw[N_G % 2][:, 0:W_G].rearrange("p (k m) -> p k m", m=RANK)
                tt(w[:, :, 1, :], raw, w[:, :, 0, :].bitcast(F32), ALU.subtract).then_inc(lo_made, 1)

            def x_rest(k, stage, gain=None):
                dve.wait_ge(xs_hi_made, stage * KT + k + 1)
                hi = xs_hi[:, k, :].bitcast(F32)
                if gain is None:
                    ins = tt(xs_lo[:, k, :], Y[:, k, :], hi, ALU.subtract)
                else:
                    ins = stt(xs_lo[:, k, :], Y[:, k, :], par(gain, k), hi, ALU.mult, ALU.subtract)
                ins.then_inc(xs_lo_made, 1)

            def add_square(n):
                dve.wait_ge(squared, n + 1)
                tt(ss[:], ss[:], sq[:], ALU.add).then_inc(sq_used, 1)
                dve.wait_ge(sq_used, n + 1)

            def newton(y, v, t):
                link(nc.vector.reciprocal(y, y))
                link(tt(t, y, y, ALU.mult))
                link(tt(t, t, v, ALU.mult))
                link(ts(t, t, -0.5, 1.5, ALU.mult, ALU.add))
                return tt(y, y, t, ALU.mult)

            def rms(n, spread, v):
                dve.wait_ge(sum_spread, n + 1)
                ts(v, spread[:], 1.0 / D, EPS, ALU.mult, ALU.add).then_inc(var_made, 1)
                dve.wait_ge(root_made, n + 1)
                newton(rstd[:], v, spread[:]).then_inc(rstd_made, 1)
                dve.wait_ge(rstd_made, n + 1)

            def rms_small(src, scale, made, root, diag, n, dst, between=None):
                v, y, t = norm4[:, 0, :], norm4[:, 1, :], norm4[:, 2, :]
                ts(v, src[:, 0:4], scale, EPS, ALU.mult, ALU.add).then_inc(made, 1)
                if between is not None:
                    between()
                dve.wait_ge(root, n)
                link(newton(y, v, t))
                tt(dst.rearrange("p (j t) -> p j t", t=P), ident[:].unsqueeze(1).to_broadcast([P, 4, P]),
                   y.unsqueeze(2).to_broadcast([P, 4, P]), ALU.mult).then_inc(diag, 1)

            def evacuate(n):
                dve.wait_ge(tile_done, n + 1)
                m = 2 * RANK if n == N_G else P
                if n < N_Q:
                    dst = Y[:, n, :]
                elif n < N_G:
                    dst = QKV[:, n - N_Q, :]
                elif n == N_G:
                    dst = g_lr[:]
                elif n < N_POOL:
                    dst = QKV[:, 8 + n - N_V, :]
                elif n < N_R:
                    dst = Y[:, 4 + n - N_POOL, :]
                else:
                    if n == N_R + 4:
                        dve.wait_ge(pooled, POOL_TILES)
                    if n == N_R + 6:
                        dve.wait_ge(pool_mixed, POOL_TILES)
                    dst = Y[:, 8 + n - N_R, :]
                tt(dst, bank[in_bank(n)][0:m, :], rstd[0:m, :], ALU.mult).then_inc(evacuated, 1)

            def u_rest(c):
                dve.wait_ge(u_hi_made, c + 1)
                tt(U[:, 6 + c % 2, :], Y[:, c, :], U[:, 4 + c % 2, :].bitcast(F32), ALU.subtract).then_inc(u_lo_made, 1)

            def find_turns(i):
                col = [s5s[:, k, i:i + 1] for k in (6, 7, 8)]
                if i == 0:
                    dve.wait_ge(step_split, 1)
                else:
                    dve.wait_ge(trig_made, i)
                link(ts(turns, iota_t, col[0], TO_INT, ALU.mult, ALU.add))
                link(ts(turns, turns, TO_INT, None, ALU.subtract))
                link(stt(turns, iota_t, col[1], turns, ALU.mult, ALU.subtract))
                link(stt(turns, iota_t, col[2], turns, ALU.mult, ALU.add))
                ts(turns, turns, 0.5, -0.5, ALU.min, ALU.max).then_inc(turns_made, 1)

            def rotate_scan(i):
                cos, sin, re, im = cos_t[i % 2], sin_t[i % 2], v_re[i % 2], v_im[i % 2]
                b_re, b_im = bank[2 + 2 * (i % 2)][:], bank[3 + 2 * (i % 2)][:]
                size = s5s[:, 3, i:i + 1].to_broadcast([P, SEQ])
                if i == 0:
                    dve.wait_ge(size_made, 1)
                dve.wait_ge(trig_made, i + 1)
                link(ts(cos, cos, -2.0, 1.0, ALU.mult, ALU.add))
                dve.wait_ge(bu_made, i + 1)
                tt(re, b_re, cos, ALU.mult)
                tt(im, b_im, cos, ALU.mult)
                link(tt(prod[:], b_im, sin, ALU.mult))
                link(tt(re, re, prod[:], ALU.add))
                tt(prod[:], b_re, sin, ALU.mult).then_inc(rotated_in, 1)
                dve.wait_ge(rotated_in, i + 1)
                link(tt(im, im, prod[:], ALU.subtract))
                nc.vector.tensor_tensor_scan(re, size, re, 0.0, ALU.mult, ALU.add)
                nc.vector.tensor_tensor_scan(im, size, im, 0.0, ALU.mult, ALU.add).then_inc(scanned, 1)

            def add_skip(c):
                dve.wait_ge(states_read, 4 * c + 4)
                stt(Y[:, c, :], Y[:, c, :], par("d", c), bank[6 + c % 2][:], ALU.mult, ALU.add).then_inc(y_added, 1)

            def head_gate(h):

                def chunks(a):
                    return a.rearrange("p (n t) -> p n t", t=CHUNK)

                dve.wait_ge(soft_made, h + 1)
                link(stt(log_a[:], log_a[:], 0.0, e_buf[:], ALU.min, ALU.subtract))
                for c in range(CHUNKS):
                    ts_ = slice(c * CHUNK, (c + 1) * CHUNK)
                    m = nc.vector.tensor_tensor_scan(log_a[:, ts_], ones[:, 0:CHUNK], log_a[:, ts_], 0.0, ALU.mult,
                                                     ALU.add)
                m.then_inc(b_made, 1)
                dve.wait_ge(b_made, h + 1)
                last = log_a[:, CHUNK - 1:SEQ:CHUNK].unsqueeze(2).to_broadcast([P, CHUNKS, CHUNK])
                tt(chunks(k_tail), last, chunks(log_a[:]), ALU.subtract).then_inc(diff_made, 1)

            def head_scale(h):
                q, k = QKV[:, h, :], QKV[:, 4 + h, :]
                dve.wait_ge(eb_made, h + 1)
                stt(q, q, float(P) ** -0.5, e_buf[:], ALU.mult, ALU.mult)
                dve.wait_ge(ebn_made, h + 1)
                tt(k_dec[:], k, k_dec[:], ALU.mult).then_inc(kd_made, 1)
                dve.wait_ge(kd_made, h + 1)
                dve.wait_ge(ebr_made, h + 1)
                tt(k, k, k_tail, ALU.mult).then_inc(kr_made, 1)

            def head_mask(h):
                dve.wait_ge(scores_made, h + 1)
                mask = causal[:].unsqueeze(1).to_broadcast([P, 4, P])
                nc.vector.copy_predicated(sc[:], mask, bank[5][:].rearrange("p (j t) -> p j t",
                                                                            j=4)).then_inc(sc_masked, 1)

            def head_state(h):
                dve.wait_ge(kv_made, h + 1)
                dve.wait_ge(decay_made, h + 1)
                for c in range(CHUNKS - 1):
                    kv = kv_place(c)
                    if c == 0:
                        ins = nc.vector.tensor_copy(S[:, 0, :], kv)
                    else:
                        ins = stt(S[:, c, :], S[:, c - 1, :], decay[:, c:c + 1], kv, ALU.mult, ALU.add)
                    if c < CHUNKS - 2:
                        link(ins)
                ins.then_inc(S_made, 1)

            def head_rms(h):
                dve.wait_ge(o_summed, h + 1)
                rms_small(bank[2], 1.0 / DV, o_var, o_root, o_diag, h + 1, QKV[:, h, :])
                if h == HEADS - 1:
                    for k in range(KT // 4):
                        x_rest(k, 1)
                dve.wait_ge(o_spread, h + 1)
                for e in range(2):
                    o = QKV[:, 8 + 2 * h + e, :]
                    m = stt(o, o, par("gla_w", e), bank[2][:], ALU.mult, ALU.mult)
                m.then_inc(o_norm, 1)
                dve.wait_ge(o_norm, h + 1)

            def gate_r(k):
                dve.wait_ge(r_silu, k + 1)
                tt(Y[:, 8 + k, :], Y[:, 8 + k, :], QKV[:, 8 + k, :], ALU.mult).then_inc(y_gla_made, 1)

            def scale_pool(g):
                dve.wait_ge(pool_mixed, g + 1)
                ts(Y[:, 4 + g, :], bank[5][:], par("pscale", g), None, ALU.mult).then_inc(y_pool_made, 1)

            nc.vector.memset(ones[:], 1.0).then_inc(ones_set, 1)
            link(nc.vector.memset(x_ss, 0.0))
            a_re, a_im, inverse, square = par("a_re", 0, PAIRS), par("a_im", 0, PAIRS), s5s[:, 13, :], s5s[:, 16, :]
            dve.wait_ge(params_in, 16)
            link(tt(inverse, a_re, a_re, ALU.mult))
            link(tt(square, a_im, a_im, ALU.mult))
            link(tt(inverse, inverse, square, ALU.add))
            nc.vector.reciprocal(inverse, inverse).then_inc(inverse_made, 1)
            for g in range(4):
                for k in range(X_GROUPS[g], X_GROUPS[g + 1]):
                    x_rest(k, 0, "mix")
                if g == 0:
                    w_rest_halves(0)
            w_rest_halves(1)
            for k in range(KT):
                dve.wait_ge(squared, k + 1)
                tt(x_ss, x_ss, x_sq[k % 2], ALU.add).then_inc(sq_used, 1)
                dve.wait_ge(sq_used, k + 1)
                if k == KT // 2 - 1:
                    w_rest(2)
            dve.wait_ge(s5_in, 80)
            dve.wait_ge(sum_spread, 1)
            rms_small(bank[7], 1.0 / D, var_made, root_made, diag_made, 1, x_diag, between=lambda: w_rest(3))
            dve.wait_ge(rstd_made, 1)
            evacuate(0)
            evacuate(1)
            for n in range(2, IN_TILES):
                s = n - HEAD_SLOT
                if s == 3:
                    dve.wait_ge(glu_sig, 4)
                    for j in range(4):
                        tt(Y[:, j, :], Y[:, j, :], glu_gate[j], ALU.mult).then_inc(y_s5_made, 1)
                    dve.wait_ge(y_s5_made, 4)
                if s in (5, 7, 9, 10):
                    head_rms((s - 5) // 2 if s < 10 else 3)
                if s in (5, 7):
                    scale_pool(s - 4)
                if n == IN_TILES - 1:
                    x_rest(KT // 4, 1)
                    x_rest(KT // 4 + 1, 1)
                evacuate(n)
                if s in (2, 4, 6, 8):
                    head_state((s - 2) // 2)
                if s in (4, 6):
                    scale_pool(s - 4)
                if s == 0:
                    dve.wait_ge(y_added, 4)
                    nc.vector.memset(sc[:], 0.0).then_inc(sc_zeroed, 1)
                    dve.wait_ge(sc_zeroed, 1)
                if s in (0, 2, 4, 6):
                    head_gate(s // 2)
                if n + 2 == N_G:
                    w_rest_rank()
                elif n < IN_TILES - 1:
                    w_rest(n + 2)
                if n == 3:
                    for c in range(2):
                        dve.wait_ge(bt_hi_made, c + 1)
                        tt(BT_lo[c][:], bank[4 + c][:].rearrange("p (j d) -> p j d", j=4),
                           BT_hi[c][:].bitcast(F32), ALU.subtract).then_inc(bt_made, 1)
                if n in U_SLOTS:
                    u_rest(U_SLOTS.index(n))
                if BU_SLOT - 1 <= n < BU_SLOT - 1 + PAIRS:
                    find_turns(n - BU_SLOT + 1)
                if BU_SLOT <= n < BU_SLOT + PAIRS:
                    rotate_scan(n - BU_SLOT)
                if READ_SLOT + 3 <= n < READ_SLOT + PAIRS and (n - READ_SLOT) % 4 == 3:
                    add_skip((n - READ_SLOT) // 4)
                if s in (0, 2, 4, 6):
                    head_scale(s // 2)
                if s in (1, 3, 5, 7):
                    head_mask((s - 1) // 2)
                if s in (5, 7, 9):
                    gate_r(s - 5)
                    gate_r(s - 4)
            for k in range(KT // 4 + 2, KT):
                x_rest(k, 1)
            w_rest(IN_TILES + 1)
            link(nc.vector.memset(ss[:], 0.0))

            def add_x(j_pair, r, s, follow, square=True):
                i = 2 * j_pair + r
                j = 2 * i + s
                if s == 0:
                    dve.wait_ge(xres_in[r], 16 * j_pair + 16)
                dve.wait_ge(tile_done, j + (OUT0 + 1))
                row = (lambda a: a[:, j, :]) if isinstance(i, int) else (lambda a: a[:, bass.ds(j, 1), :])
                out = bank[(OUT0 + s) % 2][:] if isinstance(i, int) else bank[(OUT0 + s) % 2][:].unsqueeze(1)
                tt(row(Y), row(x_res), out, ALU.add).then_inc(evacuated, 1)
                if follow is not None:
                    w_rest(*follow)
                if square:
                    add_square(j + KT)

            with dve.Fori(0, KT // 4 - 1) as j:
                for r in range(2):
                    for s in range(2):
                        add_x(j, r, s, (OUT0 + 2 + s, 2 * j + r))
            for s in range(2):
                add_x(KT // 4 - 1, 0, s, (OUT0 + 2 + s, KT // 2 - 2))
            add_x(KT // 4 - 1, 1, 0, (FFN0,))
            for k in range(KT // 2):
                x_rest(k, 2, "ffn")
            add_x(KT // 4 - 1, 1, 1, None, square=False)
            for k in range(KT // 2, KT):
                x_rest(k, 2, "ffn")
                if k == KT // 2 + 1:
                    add_square(2 * KT - 1)
            w_rest(FFN0 + 1)
            link(nc.vector.memset(conv_in[:], 0.0))
            dve.wait_ge(sum_spread, 2)
            rms_small(bank[2], 1.0 / D, var_made, root_made, diag_made, 2, val[:])
            dve.wait_ge(rstd_made, 2)

            def up_pair(q, i, width):
                e, f = q * HALF_Q + i, q * QT + i
                n = PER_QUARTER * q + 2 * i
                dve.wait_ge(tile_done, n + (FFN0 + 1))
                tt(conv_in[:, 2:], bank[FFN0 % 2][:], rstd[:], ALU.mult).then_inc(evacuated, 1)
                w_rest(FFN0 + 2, e, width)
                dve.wait_ge(evacuated, n + (FFN0 + 1))
                link(ts(conv_acc[:], conv_in[:, 2:], par("conv_w", 3 * f + 2), par("conv_b", f), ALU.mult, ALU.add))
                link(stt(conv_acc[:], conv_in[:, 1:SEQ + 1], par("conv_w", 3 * f + 1), conv_acc[:], ALU.mult, ALU.add))
                stt(conv_acc[:], conv_in[:, 0:SEQ], par("conv_w", 3 * f), conv_acc[:], ALU.mult,
                    ALU.add).then_inc(conv_made, 1)
                dve.wait_ge(conv_made, f + 1)
                dve.wait_ge(tile_done, n + (FFN0 + 2))
                tt(val[:], bank[(FFN0 + 1) % 2][:], rstd[:], ALU.mult).then_inc(evacuated, 1)
                dve.wait_ge(evacuated, n + (FFN0 + 2))
                dve.wait_ge(silu_made, f + 1)
                tt(val[:], val[:], silu_g[:], ALU.mult).then_inc(mid_made, 1)
                dve.wait_ge(mid_hi_made, f + 1)
                if isinstance(i, int):
                    hi, lo, v = mid_hi[:, i, :], mid_lo[:, i, :], val[:]
                else:
                    hi, lo = mid_hi[:, bass.ds(i, 1), :], mid_lo[:, bass.ds(i, 1), :]
                    v = val[:].unsqueeze(1)
                tt(lo, v, hi.bitcast(F32), ALU.subtract).then_inc(mid_lo_made, 1)
                dve.wait_ge(mid_lo_made, f + 1)
                w_rest(FFN0 + 3, e, width)

            def add_down(q, i, s, follow, width):
                j = 2 * i + s
                n = PER_QUARTER * q + j
                dve.wait_ge(tile_done, n + (FFN0 + UP + 1))
                out = bank[(FFN0 + UP + s) % 2][:]
                if isinstance(i, int):
                    y = Y[:, j, :]
                else:
                    y, out = Y[:, bass.ds(j, 1), :], out.unsqueeze(1)
                tt(y, y, out, ALU.add).then_inc(evacuated, 1)
                w_rest(follow, q * HALF_Q + (i if width == W_DOWN else 0), width)
                add_square(KT * q + j + 2 * KT)

            def quarter(q, last):
                with repeat(dve, QT - 1, links=(links, 2)) as i:
                    up_pair(q, i, W_FULL)
                link(nc.vector.memset(ss[:], 0.0))
                up_pair(q, QT - 1, W_DOWN)
                with repeat(dve, KT // 2 - 1, links=(links, 0)) as i:
                    for s in range(2):
                        add_down(q, i, s, FFN0 + UP + 2 + s, W_DOWN)
                if last:
                    for k in range(PLE_KT):
                        dve.wait_ge(p_hi_made, k + 1)
                        tt(p_lo[:, k, :], p_raw[k], p_hi[:, k, :].bitcast(F32), ALU.subtract).then_inc(p_lo_made, 1)
                for s in range(2):
                    add_down(q, KT // 2 - 1, s, FFN0 + PER_QUARTER + s, W_FULL)

            with repeat(dve, QUARTERS - 1, links=(links, 2 * QT + 1)) as q:
                quarter(q, False)
            quarter(QUARTERS - 1, True)

            for k in range(KT):
                x_rest(k, 3, "ple")
                if k == 10:
                    w_rest(PG0)
            w_rest(PG0 + 1)
            rms(2, bank[2], val[:])
            link(nc.vector.memset(ss[:], 0.0))

            def add_gated(i, s, follow, square=True):
                j = 2 * i + s
                dve.wait_ge(tile_done, j + (PG0 - 2 + 1))
                tt(conv_acc[:], bank[(PG0 + s) % 2][:], rstd[:], ALU.mult).then_inc(evacuated, 1)
                if follow is not None:
                    w_rest(*follow)
                if isinstance(i, int):
                    y, g, v, gate = Y[:, j, :], ple[:, j, :], val[:], conv_acc[:]
                else:
                    y, g = Y[:, bass.ds(j, 1), :], ple[:, bass.ds(j, 1), :]
                    v, gate = val[:].unsqueeze(1), conv_acc[:].unsqueeze(1)
                dve.wait_ge(gate_made, j + 1)
                link(tt(v, gate, g, ALU.mult))
                tt(y, y, v, ALU.add).then_inc(h_made, 1)
                if square:
                    dve.wait_ge(h_made, j + 1)
                    add_square(j + (2 + QUARTERS) * KT)

            with repeat(dve, KT // 2 - 1, links=(links, 2)) as i:
                for s in range(2):
                    add_gated(i, s, (PG0 + 2 + s, i))
            for s in range(2):
                add_gated(KT // 2 - 1, s, None, square=s == 0)
            dve.wait_ge(sum_spread, 4)
            rms_small(bank[2], 1.0 / D, var_made, root_made, diag_made, 4, val[:])
            dve.wait_ge(rstd_made, 4)
            for j in range(POOL_OUT, KT):
                stt(Y[:, j, :], Y[:, j, :], par("final", j), rstd[:], ALU.mult, ALU.mult).then_inc(out_made, 1)

        @block.gpsimd
        def _(pool):
            tt, ts = nc.gpsimd.tensor_tensor, nc.gpsimd.tensor_scalar
            links = Count(p_link)

            def link(ins):
                pool.wait_ge(p_link, links.inc(ins))

            def s5_constants():
                a_re, a_im = par("a_re", 0, PAIRS), par("a_im", 0, PAIRS)
                c = [s5s[:, k, :] for k in range(17)]
                pool.wait_ge(params_in, 16)
                pool.wait_ge(dt_made, 1)
                tt(c[1], a_re, c[0], ALU.mult).then_inc(exp_in, 1)
                link(tt(c[2], a_im, c[0], ALU.mult))
                link(ts(c[4], c[2], INV_2PI, TO_INT, ALU.mult, ALU.add))
                link(ts(c[4], c[4], TO_INT, None, ALU.subtract))
                link(ts(c[12], c[4], -PI2_A, None, ALU.mult))
                link(tt(c[5], c[12], c[2], ALU.add))
                link(ts(c[12], c[4], -PI2_B, None, ALU.mult))
                link(tt(c[5], c[12], c[5], ALU.add))
                link(ts(c[12], c[4], -PI2_C, None, ALU.mult))
                link(tt(c[5], c[12], c[5], ALU.add))
                link(ts(c[6], c[5], INV_2PI, 0.5, ALU.mult, ALU.min))
                ts(c[6], c[6], -0.5, None, ALU.max).then_inc(step_turns, 1)
                pool.wait_ge(step_turns, 1)
                link(ts(c[7], c[6], TO_2_16, None, ALU.add))
                link(ts(c[7], c[7], TO_2_16, None, ALU.subtract))
                tt(c[8], c[6], c[7], ALU.subtract).then_inc(step_split, 1)
                pool.wait_ge(step_trig, 1)
                pool.wait_ge(size_made, 1)
                link(tt(c[10], c[10], c[10], ALU.mult))
                link(ts(c[10], c[10], -2.0, 1.0, ALU.mult, ALU.add))
                link(tt(c[11], c[3], c[10], ALU.mult))
                link(tt(c[12], c[3], c[9], ALU.mult))
                link(ts(c[11], c[11], -1.0, None, ALU.add))
                pool.wait_ge(inverse_made, 1)
                link(tt(c[14], c[11], a_re, ALU.mult))
                link(tt(c[15], c[12], a_im, ALU.mult))
                link(tt(c[14], c[14], c[15], ALU.add))
                link(tt(c[14], c[14], c[13], ALU.mult))
                link(tt(c[15], c[12], a_re, ALU.mult))
                link(tt(c[16], c[11], a_im, ALU.mult))
                link(tt(c[15], c[15], c[16], ALU.subtract))
                link(tt(c[15], c[15], c[13], ALU.mult))
                pool.wait_ge(s5_in, 80)

                def blocks(a):
                    return a.rearrange("p (i c) -> p i c", c=32)

                f = [c[14 + z].unsqueeze(2).to_broadcast([P, PAIRS, 32]) for z in range(2)]
                link(tt(blocks(B_bar[0]), blocks(B_in[0]), f[0], ALU.mult))
                link(tt(blocks(B_prod), blocks(B_in[1]), f[1], ALU.mult))
                link(tt(B_bar[0], B_bar[0], B_prod, ALU.subtract))
                link(tt(blocks(B_bar[1]), blocks(B_in[1]), f[0], ALU.mult))
                link(tt(blocks(B_prod), blocks(B_in[0]), f[1], ALU.mult))
                tt(B_bar[1], B_bar[1], B_prod, ALU.add).then_inc(bbar_made, 1)
                ts(CM[:, 1, :, :], CM[:, 1, :, :], -1.0, None, ALU.mult).then_inc(cm_made, 1)

            s5_constants()
            for i in range(PAIRS):
                cos, sin, re, im = cos_t[i % 2], sin_t[i % 2], v_re[i % 2], v_im[i % 2]
                pool.wait_ge(scanned, i + 1)
                if i >= 1:
                    pool.wait_ge(states_read, i)
                tt(st_re[:], re, cos, ALU.mult)
                link(tt(st_t[:], im, sin, ALU.mult))
                link(tt(st_re[:], st_re[:], st_t[:], ALU.subtract))
                tt(st_im[:], re, sin, ALU.mult)
                link(tt(st_t[:], im, cos, ALU.mult))
                tt(st_im[:], st_im[:], st_t[:], ALU.add).then_inc(states_made, 1)
                pool.wait_ge(states_made, i + 1)

            pool.wait_ge(a2_in, 48)
            pool.wait_ge(glu_done, 4)
            for g in range(POOL_TILES):
                pool.wait_ge(evacuated, N_POOL + g + 1)
                z = Y[:, 4 + g, :]
                src = z
                for k in range(g + 1):
                    sh, dst = 2 ** k, window[k % 2]
                    tt(dst[:, sh:], src[:, sh:], src[:, 0:SEQ - sh], ALU.add)
                    link(nc.gpsimd.tensor_copy(dst[:, 0:sh], src[:, 0:sh]))
                    src = dst
                link(nc.gpsimd.tensor_scalar(src, src, 0.5 ** (g + 1), None, ALU.mult))
                link(tt(src[:, 0:16], src[:, 0:16], corr[:, g, :], ALU.mult))
                tt(z, src, z, ALU.subtract).then_inc(pooled, 1)
                pool.wait_ge(pooled, g + 1)

            pool.wait_ge(o_norm, HEADS)
            for k in (6, 7):
                pool.wait_ge(r_silu, k + 1)
                tt(Y[:, 8 + k, :], Y[:, 8 + k, :], QKV[:, 8 + k, :], ALU.mult).then_inc(y_gla_made, 1)

            pool.wait_ge(scaled, POOL_OUT)
            pool.wait_ge(rstd_made, 4)
            for j in range(POOL_OUT):
                tt(Y[:, j, :], Y[:, j, :], rstd[:], ALU.mult).then_inc(out_pool_made, 1)


INPUTS = ["x", "p", "params", "ident", "corr", "iota", "causal", "s5_b", "s5_c", "w_in", "w_in_g", "w_a2", "w_glu",
          "w_pool", "w_out", "w_up", "w_down", "w_ple", "w_pg"]


def lay_out(x, p, norm_mix_w, w_in, s5_a_re, s5_a_im, s5_log_dt, s5_b_re, s5_b_im, s5_c_re, s5_c_im, s5_d,
            s5_w_glu, s5_b_glu, pool_w, pool_scale, gla_w_a2, gla_b_a, gla_norm_w, w_out, norm_ffn_w, w_up,
            conv_w, conv_b, w_down, norm_ple_w, w_ple, w_pg, final_norm_w):
    import numpy as np

    def tiles(w, m=P):
        k, n = w.shape
        return w.reshape(k // P, P, n // m, m).transpose(2, 1, 0, 3).reshape(n // m, P, k // P * m)

    def cols(v):
        return v.reshape(-1, P).T

    def features(a):
        return a.T.reshape(-1, P, a.shape[0]).transpose(1, 0, 2)

    out = {"x": features(x[0]), "p": features(p[0, 0])}
    wi = w_in[0]
    order = [(0, 512), (1024, 1536), (1536, 2048), (2048, 3072), (512, 1024), (3088, 4112)]
    out["w_in"] = tiles(np.concatenate([wi[:, a:b] for a, b in order], axis=1))
    out["w_in_g"] = tiles(wi[:, 3072:3088], RANK)[0]
    out["w_out"] = tiles(w_out[0])
    up = w_up[0]
    out["w_up"] = np.stack([tiles(up[:, :D_FF]), tiles(up[:, D_FF:])], axis=1).reshape(2 * FT, P, D)
    out["w_down"] = np.concatenate([tiles(w_down[0][q * QT * P:(q + 1) * QT * P]) for q in range(QUARTERS)])
    out["w_pg"] = tiles(w_pg[0])
    out["w_ple"] = tiles(w_ple[0]).reshape(2, PLE_PER, P, PLE_KT * P).transpose(0, 2, 1, 3).reshape(2, P, D)
    out["w_glu"] = s5_w_glu[0].reshape(S5_TILES, P, SEQ).transpose(1, 0, 2)
    out["w_pool"] = pool_w[0].transpose(1, 0, 2).reshape(P, POOL_TILES * P)
    out["w_a2"] = np.concatenate([gla_w_a2[0]] * 2)

    def states(a):
        return a.reshape(PAIRS, 2 * STATES).T

    dt = np.repeat(s5_log_dt[0][:, None], STATES, axis=1)
    out["params"] = np.concatenate(
        [cols(norm_mix_w[0]), cols(norm_ffn_w[0]), cols(norm_ple_w[0]), cols(final_norm_w), cols(s5_d[0]),
         cols(s5_b_glu[0]), cols(pool_scale[0]), cols(gla_b_a[0]), cols(gla_norm_w[0]), cols(conv_b[0]),
         conv_w[0].reshape(3, FT, P).transpose(2, 1, 0).reshape(P, 3 * FT), states(s5_a_re[0]),
         states(s5_a_im[0]), states(dt)], axis=1)

    def blocks(a):
        b = np.zeros((2, STATES, PAIRS, 2, 16), a.dtype)
        for g in range(2):
            b[g, :, :, g, :] = a[g::2].transpose(1, 0, 2)
        return b.reshape(P, 1, PAIRS, 32)

    out["s5_b"] = np.concatenate([blocks(s5_b_re[0]), blocks(s5_b_im[0])], axis=1).reshape(P, 2, SEQ)
    out["s5_c"] = np.concatenate([blocks(s5_c_re[0].transpose(0, 2, 1)), blocks(s5_c_im[0].transpose(0, 2, 1))],
                                 axis=1)
    corr = [[2.0 ** (g + 1) / min(t + 1, 2 ** (g + 1)) for t in range(16)] for g in range(POOL_TILES)]
    corr = np.broadcast_to(np.array(corr, np.float32).reshape(1, 64), (P, 64))
    out["corr"] = corr.reshape(P, POOL_TILES, 16)
    out["ident"] = np.eye(P, dtype=np.float32)
    out["iota"] = np.broadcast_to(np.arange(SEQ, dtype=np.float32), (P, SEQ))
    s, t = np.arange(P)[:, None], np.arange(P)[None, :]
    out["causal"] = ((s <= t) & (s // CHUNK == t // CHUNK)).astype(np.uint32)
    return {k: np.ascontiguousarray(v) for k, v in out.items()}


def kernel(**inputs):
    import numpy as np
    from concourse import bacc
    from concourse.bass_utils import run_bass_kernel_spmd

    arrays = lay_out(**{k: np.asarray(v) for k, v in inputs.items()})
    nc = bacc.Bacc("TRN2", target_bir_lowering=False, num_devices=1)
    A = {n: nc.dram_tensor(f"in_{n}", arrays[n].shape, mybir.dt.from_np(arrays[n].dtype), kind="ExternalInput").ap()
         for n in INPUTS}
    A["out"] = nc.dram_tensor("out_h", (P, KT, SEQ), F32, kind="ExternalOutput").ap()
    build(nc, A)
    r = run_bass_kernel_spmd(nc, [{f"in_{n}": arrays[n] for n in INPUTS}], core_ids=[0])
    out = r.results[0]["out_h"]
    return np.asarray(out).transpose(2, 1, 0).reshape(1, SEQ, D)
```
